# Optimizing a Trainium2 kernel written in Bass

```python
import math
import jax, jax.numpy as jnp
from jax import lax
import numpy as np

D_MODEL = 2048
BATCH = 1
SEQ = 256
DEPTH = 2

N_MIXERS = 2
N_LAYERS_A = (DEPTH + 1) // 2
N_LAYERS_B = DEPTH // 2
NORM_EPS = 1e-6
PLE_DIM = 256
D_FF = -(-8 * D_MODEL // (3 * 256)) * 256
LRU_WIDTH = D_MODEL
LRU_HEADS = 8
LRU_BLOCK = LRU_WIDTH // LRU_HEADS
CONV_WIDTH = 4
LRU_C = 8.0
SSD_EXPAND = 2
SSD_INNER = SSD_EXPAND * D_MODEL
SSD_HEAD_DIM = 64
SSD_HEADS = SSD_INNER // SSD_HEAD_DIM
SSD_GROUPS = 8
SSD_HEADS_PER_GROUP = SSD_HEADS // SSD_GROUPS
SSD_STATE = 128
SSD_CHUNK = 128
SSD_CONV_DIM = SSD_INNER + 2 * SSD_GROUPS * SSD_STATE
SSD_IN_DIM = SSD_INNER + SSD_CONV_DIM + SSD_HEADS
SSD_NORM_GROUP = SSD_INNER // SSD_GROUPS

kernel_name = "hybrid_rglru_ssd_swiglu_ple"

def rmsnorm(x, g):
    xf = x.astype(jnp.float32)
    y = xf * lax.rsqrt(jnp.mean(xf * xf, axis=-1, keepdims=True) + NORM_EPS)
    return (y * g.astype(jnp.float32)).astype(x.dtype)

def causal_dwconv(x, w, b):
    W = w.shape[0]
    S = x.shape[1]
    xp = jnp.pad(x, ((0, 0), (W - 1, 0), (0, 0)))
    y = b + xp[:, 0:S] * w[0]
    for k in range(1, W):
        y = y + xp[:, k:k + S] * w[k]
    return y

def _lin_combine(c1, c2):
    a1, b1 = c1
    a2, b2 = c2
    return (a1 * a2, a2 * b1 + b2)

def rglru_mixer(u, w_in, conv_w, conv_b, w_gate_r, b_gate_r, w_gate_i, b_gate_i, lam, w_out):
    bsz, S, _ = u.shape
    xy = u @ w_in
    xr, yg = jnp.split(xy, 2, axis=-1)
    yg = jax.nn.gelu(yg, approximate=True)
    xr = causal_dwconv(xr, conv_w, conv_b)
    xb = xr.reshape(bsz, S, LRU_HEADS, LRU_BLOCK)
    r = jax.nn.sigmoid(jnp.einsum('bshi,hij->bshj', xb, w_gate_r) + b_gate_r).reshape(bsz, S, LRU_WIDTH)
    i = jax.nn.sigmoid(jnp.einsum('bshi,hij->bshj', xb, w_gate_i) + b_gate_i).reshape(bsz, S, LRU_WIDTH)
    log_a = -LRU_C * r.astype(jnp.float32) * jax.nn.softplus(-lam.astype(jnp.float32))
    a = jnp.exp(log_a)
    mult = jnp.sqrt(-jnp.expm1(2.0 * log_a))
    bterm = mult * (i * xr).astype(jnp.float32)
    _, hs = lax.associative_scan(_lin_combine, (a, bterm), axis=1)
    y = hs.astype(u.dtype) * yg
    return y @ w_out

def segsum(x):
    T = x.shape[-1]
    cs = jnp.cumsum(x, axis=-1)
    diff = cs[..., :, None] - cs[..., None, :]
    mask = jnp.tril(jnp.ones((T, T), dtype=bool))
    return jnp.where(mask, diff, -jnp.inf)

def ssd_scan(x, dt, A, Bm, Cm):
    b, S, H, P = x.shape
    L = SSD_CHUNK
    nc = S // L
    G, E, N = SSD_GROUPS, SSD_HEADS_PER_GROUP, SSD_STATE
    X = (x * dt[..., None]).reshape(b, nc, L, G, E, P)
    Adt = (A * dt).reshape(b, nc, L, G, E).transpose(0, 3, 4, 1, 2)
    Bc = Bm.reshape(b, nc, L, G, N)
    Cc = Cm.reshape(b, nc, L, G, N)
    A_cs = jnp.cumsum(Adt, axis=-1)
    Lmat = jnp.exp(segsum(Adt))
    CB = jnp.einsum('bclgn,bcsgn->bgcls', Cc, Bc)
    scores = CB[:, :, None] * Lmat
    y_diag = jnp.einsum('bgecls,bcsgep->bclgep', scores, X)
    decay_states = jnp.exp(A_cs[..., -1:] - A_cs)
    states = jnp.einsum('bclgn,bgecl,bclgep->bcgepn', Bc, decay_states, X)
    states = jnp.concatenate([jnp.zeros_like(states[:, :1]), states], axis=1)
    chunk_tot = jnp.pad(A_cs[..., -1], ((0, 0), (0, 0), (0, 0), (1, 0)))
    decay_chunk = jnp.exp(segsum(chunk_tot))
    states_in = jnp.einsum('bgezc,bcgepn->bzgepn', decay_chunk, states)[:, :-1]
    y_off = jnp.einsum('bclgn,bcgepn,bgecl->bclgep', Cc, states_in, jnp.exp(A_cs))
    return (y_diag + y_off).reshape(b, S, H, P)

def ssd_mixer(u, w_in, conv_w, conv_b, dt_bias, a_log, d_skip, norm_g, w_out):
    b, S, _ = u.shape
    G, N = SSD_GROUPS, SSD_STATE
    zxbcdt = u @ w_in
    z = zxbcdt[..., :SSD_INNER]
    xbc = zxbcdt[..., SSD_INNER:SSD_INNER + SSD_CONV_DIM]
    dt = zxbcdt[..., SSD_INNER + SSD_CONV_DIM:]
    xbc = jax.nn.silu(causal_dwconv(xbc, conv_w, conv_b))
    xs = xbc[..., :SSD_INNER].reshape(b, S, SSD_HEADS, SSD_HEAD_DIM).astype(jnp.float32)
    Bm = xbc[..., SSD_INNER:SSD_INNER + G * N].reshape(b, S, G, N).astype(jnp.float32)
    Cm = xbc[..., SSD_INNER + G * N:].reshape(b, S, G, N).astype(jnp.float32)
    dt = jax.nn.softplus(dt.astype(jnp.float32) + dt_bias.astype(jnp.float32))
    A = -jnp.exp(a_log.astype(jnp.float32))
    y = ssd_scan(xs, dt, A, Bm, Cm)
    y = y + d_skip.astype(jnp.float32)[:, None] * xs
    y = y.reshape(b, S, SSD_INNER) * jax.nn.silu(z.astype(jnp.float32))
    yg = y.reshape(b, S, SSD_GROUPS, SSD_NORM_GROUP)
    yg = yg * lax.rsqrt(jnp.mean(yg * yg, axis=-1, keepdims=True) + NORM_EPS)
    y = (yg.reshape(b, S, SSD_INNER) * norm_g.astype(jnp.float32)).astype(u.dtype)
    return y @ w_out

def swiglu(u, w_gate, w_up, w_down):
    return (jax.nn.silu(u @ w_gate) * (u @ w_up)) @ w_down

def setup_inputs(seed: int = 0) -> dict:
    key = jax.random.key(seed)
    ks = jax.random.split(key, 32)
    f32 = jnp.float32
    nrm = lambda k, shape, scale: jax.random.normal(k, shape, f32) * scale
    gain = lambda k, shape: 1.0 + 0.02 * jax.random.normal(k, shape, f32)
    x = jax.random.normal(ks[0], (BATCH, SEQ, D_MODEL), f32)
    p = jax.random.normal(ks[1], (DEPTH, BATCH, SEQ, PLE_DIM), f32)
    norm_mix_g = gain(ks[2], (DEPTH, D_MODEL))
    norm_ffn_g = gain(ks[3], (DEPTH, D_MODEL))
    norm_ple_g = gain(ks[4], (DEPTH, D_MODEL))
    final_norm_g = gain(ks[5], (D_MODEL,))
    a_w_in = nrm(ks[6], (N_LAYERS_A, D_MODEL, 2 * LRU_WIDTH), D_MODEL ** -0.5)
    a_conv_w = nrm(ks[7], (N_LAYERS_A, CONV_WIDTH, LRU_WIDTH), CONV_WIDTH ** -0.5)
    a_conv_b = nrm(ks[8], (N_LAYERS_A, LRU_WIDTH), 0.01)
    a_w_gate_r = nrm(ks[9], (N_LAYERS_A, LRU_HEADS, LRU_BLOCK, LRU_BLOCK), LRU_BLOCK ** -0.5)
    a_b_gate_r = nrm(ks[10], (N_LAYERS_A, LRU_HEADS, LRU_BLOCK), 0.01)
    a_w_gate_i = nrm(ks[11], (N_LAYERS_A, LRU_HEADS, LRU_BLOCK, LRU_BLOCK), LRU_BLOCK ** -0.5)
    a_b_gate_i = nrm(ks[12], (N_LAYERS_A, LRU_HEADS, LRU_BLOCK), 0.01)
    u_a = jax.random.uniform(ks[13], (N_LAYERS_A, LRU_WIDTH), f32, 0.9, 0.999)
    s_a = u_a ** (1.0 / LRU_C)
    a_lambda = jnp.log(s_a) - jnp.log1p(-s_a)
    a_w_out = nrm(ks[14], (N_LAYERS_A, LRU_WIDTH, D_MODEL), LRU_WIDTH ** -0.5)
    b_w_in = nrm(ks[15], (N_LAYERS_B, D_MODEL, SSD_IN_DIM), D_MODEL ** -0.5)
    b_conv_w = nrm(ks[16], (N_LAYERS_B, CONV_WIDTH, SSD_CONV_DIM), CONV_WIDTH ** -0.5)
    b_conv_b = nrm(ks[17], (N_LAYERS_B, SSD_CONV_DIM), 0.01)
    dt0 = jnp.exp(jax.random.uniform(ks[18], (N_LAYERS_B, SSD_HEADS), f32, math.log(1e-3), math.log(1e-1)))
    b_dt_bias = dt0 + jnp.log(-jnp.expm1(-dt0))
    b_a_log = jnp.log(jax.random.uniform(ks[19], (N_LAYERS_B, SSD_HEADS), f32, 1.0, 16.0))
    b_d_skip = 1.0 + 0.1 * jax.random.normal(ks[20], (N_LAYERS_B, SSD_HEADS), f32)
    b_norm_g = gain(ks[21], (N_LAYERS_B, SSD_INNER))
    b_w_out = nrm(ks[22], (N_LAYERS_B, SSD_INNER, D_MODEL), SSD_INNER ** -0.5)
    ffn_w_gate = nrm(ks[23], (DEPTH, D_MODEL, D_FF), D_MODEL ** -0.5)
    ffn_w_up = nrm(ks[24], (DEPTH, D_MODEL, D_FF), D_MODEL ** -0.5)
    ffn_w_down = nrm(ks[25], (DEPTH, D_FF, D_MODEL), D_FF ** -0.5)
    ple_w_proj = nrm(ks[26], (DEPTH, PLE_DIM, D_MODEL), PLE_DIM ** -0.5)
    ple_w_gate = nrm(ks[27], (DEPTH, D_MODEL, D_MODEL), D_MODEL ** -0.5)
    return {"x": x, "p": p, "norm_mix_g": norm_mix_g, "norm_ffn_g": norm_ffn_g,
            "norm_ple_g": norm_ple_g, "final_norm_g": final_norm_g,
            "a_w_in": a_w_in, "a_conv_w": a_conv_w, "a_conv_b": a_conv_b,
            "a_w_gate_r": a_w_gate_r, "a_b_gate_r": a_b_gate_r,
            "a_w_gate_i": a_w_gate_i, "a_b_gate_i": a_b_gate_i,
            "a_lambda": a_lambda, "a_w_out": a_w_out,
            "b_w_in": b_w_in, "b_conv_w": b_conv_w, "b_conv_b": b_conv_b,
            "b_dt_bias": b_dt_bias, "b_a_log": b_a_log, "b_d_skip": b_d_skip,
            "b_norm_g": b_norm_g, "b_w_out": b_w_out,
            "ffn_w_gate": ffn_w_gate, "ffn_w_up": ffn_w_up, "ffn_w_down": ffn_w_down,
            "ple_w_proj": ple_w_proj, "ple_w_gate": ple_w_gate}

def reference(x, p, norm_mix_g, norm_ffn_g, norm_ple_g, final_norm_g,
              a_w_in, a_conv_w, a_conv_b, a_w_gate_r, a_b_gate_r, a_w_gate_i, a_b_gate_i,
              a_lambda, a_w_out,
              b_w_in, b_conv_w, b_conv_b, b_dt_bias, b_a_log, b_d_skip, b_norm_g, b_w_out,
              ffn_w_gate, ffn_w_up, ffn_w_down, ple_w_proj, ple_w_gate):
    h = x
    for i in range(DEPTH):
        u = rmsnorm(h, norm_mix_g[i])
        j = i // N_MIXERS
        if i % N_MIXERS == 0:
            m = rglru_mixer(u, a_w_in[j], a_conv_w[j], a_conv_b[j], a_w_gate_r[j], a_b_gate_r[j],
                            a_w_gate_i[j], a_b_gate_i[j], a_lambda[j], a_w_out[j])
        else:
            m = ssd_mixer(u, b_w_in[j], b_conv_w[j], b_conv_b[j], b_dt_bias[j], b_a_log[j],
                          b_d_skip[j], b_norm_g[j], b_w_out[j])
        h = h + m
        h = h + swiglu(rmsnorm(h, norm_ffn_g[i]), ffn_w_gate[i], ffn_w_up[i], ffn_w_down[i])
        gate = jax.nn.sigmoid(rmsnorm(h, norm_ple_g[i]) @ ple_w_gate[i])
        h = h + gate * (p[i].astype(h.dtype) @ ple_w_proj[i])
    return rmsnorm(h, final_norm_g)


_drawn_inputs = setup_inputs


def setup_inputs(seed=0):
    import zlib

    import numpy as np

    out = dict(_drawn_inputs(seed))
    spreads = {}
    factors = {'norm_ffn_g': 3.036,
     'norm_ple_g': 64.0,
     'final_norm_g': 7.532,
     'a_b_gate_r': 40.772,
     'a_b_gate_i': 22.841,
     'b_conv_b': 6.804,
     'b_norm_g': 18.019}
    for name, (base, spread) in spreads.items():
        noise = np.random.default_rng([zlib.crc32(name.encode()), seed]).standard_normal(out[name].shape)
        drawn = base * np.exp(spread * noise) if base else spread * noise
        out[name] = __import__('jax').numpy.asarray(drawn.astype(out[name].dtype))
    for name, factor in factors.items():
        out[name] = (out[name] * factor).astype(out[name].dtype)
    return out
```

```python
from contextlib import ExitStack

import concourse.bass as bass
from concourse import mybir

F32 = mybir.dt.float32
F32R = mybir.dt.float32r
ALU = mybir.AluOpType
ACT = mybir.ActivationFunctionType

P = 128
SEQ = 256
D = 2048
KT = D // P
EPS = 1e-6
ARENA = 11464
FF_TILES = 44
HALF = FF_TILES // 2
LRU_HEADS = 8
GROUPS = 8
HEADS = 64
GROUP_HEADS = HEADS // GROUPS
CHUNK = 128
RING = 4
LEAD = 3
BLOCK = P
PIECE = 8
GELU_C = 0.7978845608028654
BANKS4 = [2, 3, 0, 1]
BANKS2 = [0, 1]

GAINS = 7 * KT
A_PAR = 8
B_PAR = 38


def phase_table():
    t = [("A1", 0, 0, 4, [8] * 16, 8), ("A2", 0, 0, 4, [8] * 8, 4)]
    for layer in range(2):
        if layer == 1:
            for half in range(2):
                t.append(("B1", 1, half, 4, [8] * 20, 10))
                t.append(("B2", 1, half, 4, [8] * 8, 4))
        for half in range(2):
            t.append(("F1", layer, half, HALF // 2, [8] * 8, 4))
            t.append(("F2", layer, half, 4, [6, 5, 6, 5] * 4, 4))
        t.append(("PL", layer, 0, 8, [5, 5, 4, 4] * 2, 4))
    out, piece, group = [], 0, 0
    for name, layer, half, iters, widths, groups in t:
        out.append(dict(name=name, layer=layer, half=half, iters=iters, widths=widths, groups=groups,
                        piece0=piece, group0=group))
        piece += iters * len(widths)
        group += iters * groups
    return out


class Chain:

    def __init__(self, engine, semaphore):
        self.engine, self.semaphore, self.total = engine, semaphore, 0
        self.begin(0, 0)

    def begin(self, it, per_iteration):
        self.it, self.per, self.n = it, per_iteration, 0

    def mark(self, instruction):
        instruction.then_inc(self.semaphore, 1)
        self.n += 1
        return self.total + self.it * self.per + self.n

    def need(self, value):
        self.engine.wait_ge(self.semaphore, value)

    def link(self, instruction):
        self.need(self.mark(instruction))

    def latest(self):
        return self.total + self.it * self.per + self.n

    def close(self, iterations=1):
        assert self.per in (0, self.n), (self.per, self.n)
        self.total += iterations * self.n
        self.begin(0, 0)


def trunk(nc, t, out, STOP=None):
    with ExitStack() as ctx:
        def sb(name, shape, dt=F32):
            return ctx.enter_context(nc.sbuf_tensor(name, shape, dt))

        def sem(name):
            return ctx.enter_context(nc.semaphore(name))

        h = sb("h", [P, KT, SEQ])
        R = [sb(f"R{i}", [P, 2, HALF, SEQ], F32R) for i in range(2)]
        wraw = sb("wraw", [P, RING, PIECE * BLOCK])
        whi = sb("whi", [P, RING, PIECE * BLOCK], F32R)
        wlo = sb("wlo", [P, RING, PIECE * BLOCK], F32R)
        rinv = sb("rinv", [P, SEQ])
        rinvh = sb("rinvh", [P, SEQ])
        sumsq = sb("sumsq", [P, SEQ])
        square = sb("square", [P, SEQ])
        grms = sb("grms", [P, SEQ])
        ident = sb("ident", [P, P])
        ones = sb("ones", [P, P])
        causal = sb("causal", [P, CHUNK])
        gains = sb("gains", [P, GAINS])
        apar = sb("apar", [P, KT, A_PAR])
        bpar = sb("bpar", [P, GROUPS, B_PAR])
        hpar = sb("hpar", [HEADS, 2])
        arena = sb("arena", [P, ARENA])
        used = [0]

        def scratch(n):
            a = arena[:, used[0]:used[0] + n]
            used[0] += n
            assert used[0] <= ARENA
            return a

        praw = scratch(512)
        swi_g = scratch(512).rearrange("p (j t) -> p j t", j=2)
        swi_t = scratch(512).rearrange("p (j t) -> p j t", j=2)
        swi_u = scratch(512).rearrange("p (j t) -> p j t", j=2)
        keep = used[0]
        graw = scratch(2048)
        xpad = scratch(2 * 260).rearrange("p (j t) -> p j t", j=2)
        xc = scratch(1024).rearrange("p (h j t) -> p h j t", h=2, j=2)
        yv = scratch(1024).rearrange("p (h j t) -> p h j t", h=2, j=2)
        ge = scratch(512).rearrange("p (j t) -> p j t", j=2)
        tr = scratch(512).rearrange("p (j t) -> p j t", j=2)
        ti = scratch(512).rearrange("p (j t) -> p j t", j=2)
        av = scratch(512).rearrange("p (j t) -> p j t", j=2)
        sq = scratch(512).rearrange("p (j t) -> p j t", j=2)
        kt_a, kt_b, kt_c = scratch(16), scratch(16), scratch(16)
        sumsq2, square3 = ge[:, 0, :], ge[:, 1, :]
        used[0] = keep
        csb = scratch(2048).rearrange("p (e t) -> p e t", e=GROUP_HEADS)
        cpad = scratch(2 * 260).rearrange("p (j t) -> p j t", j=2)
        ebc = scratch(1024).rearrange("p (e t) -> p e t", e=GROUP_HEADS)
        xtok = scratch(1024).rearrange("p (c n) -> p c n", c=2)
        ysq = xtok.rearrange("p c (j t) -> p (c j) t", j=2)
        xdec = scratch(512)
        state = scratch(512)
        ca = scratch(6 * SEQ).rearrange("p (n t) -> p n t", n=6)
        zt = scratch(4 * SEQ).rearrange("p (n t) -> p n t", n=4)
        cth = scratch(2 * SEQ).rearrange("p (n t) -> p n t", n=2)
        btok = scratch(P)
        cbm = scratch(2 * CHUNK).rearrange("p (c l) -> p c l", c=2)
        cst = scratch(2 * HEADS).rearrange("p (c e) -> p c e", c=2)
        dtt = scratch(2 * HEADS).rearrange("p (c e) -> p c e", c=2)
        wdt = scratch(HEADS)
        dt_x, dt_e, dt_w, dt_z = [xtok[0:HEADS, c, n * SEQ:(n + 1) * SEQ] for c in range(2) for n in range(2)]
        dt_r, dt_v, dt_cs, dt_one = [zt[0:HEADS, n, :] for n in range(4)]
        dt_dec = xdec[0:HEADS, 0:CHUNK]

        bank = [ctx.enter_context(nc.psum_tensor(f"bank{i}", [P, 512], F32)) for i in range(8)]

        assert used[0] <= ARENA
        cs_dram = nc.dram_tensor("cs_rows", [HEADS, SEQ], F32, kind="Internal").ap()

        params_in = sem("params_in")
        gains_in = sem("gains_in")
        x_in = [sem(f"x_in{c}") for c in range(4)]
        p_in = sem("p_in")
        w_landed = [sem(f"w_landed{i}") for i in range(RING)]
        g_landed = sem("g_landed")
        w_hi, w_lo, w_used, bank_free = sem("w_hi"), sem("w_lo"), sem("w_used"), sem("bank_free")
        g_hi, g_lo, g_used = sem("g_hi"), sem("g_lo"), sem("g_used")
        const_done = sem("const_done")
        dve_own, act_own, pool_own = sem("dve_own"), sem("act_own"), sem("pool_own")
        u0_hi = sem("u0_hi")
        uh_done, u_ready = sem("uh_done"), sem("u_ready")
        sumsq2_done = sem("sumsq2_done")
        yz_done = sem("yz_done")
        sumsq_done, stats_done, var_done, rinv_done = sem("sumsq_done"), sem("stats_done"), sem("var_done"), sem("rinv_done")
        tanh_done, mid_done, mid_hi, mid_ready = sem("tanh_done"), sem("mid_done"), sem("mid_hi"), sem("mid_ready")
        p_hi, p_lo = sem("p_hi"), sem("p_lo")
        ple_t, h_done = sem("ple_t"), sem("h_done")
        softexp_in, softexp_out = sem("softexp_in"), sem("softexp_out")
        kk_done = sem("kk_done")
        xc_done, xc_hi, xc_lo = sem("xc_done"), sem("xc_hi"), sem("xc_lo")
        gate_t, a_done, e_done, asq_done, s_done, mult_done = (sem("gate_t"), sem("a_done"), sem("e_done"),
                                                               sem("asq_done"), sem("s_done"), sem("mult_done"))
        cube_done, gelu_q, gelu_t, y_done, y_hi, y_lo = sem("cube_done"), sem("gelu_q"), sem("gelu_t"), sem("y_done"), sem("y_hi"), sem("y_lo")
        cs_done0 = sem("cs_done0")
        dt_mm, cs_done, cs_out, cs_in = sem("dt_mm"), sem("cs_done"), sem("cs_out"), sem("cs_in")
        a_exp, dec_in, dec_exp, wdec_done, col_t, col_done = (sem("a_exp"), sem("dec_in"), sem("dec_exp"),
                                                              sem("wdec_done"), sem("col_t"), sem("col_done"))
        conv_done, conv_t, silu_done = sem("conv_done"), sem("conv_t"), sem("silu_done")
        z_t, ebc_done, exp_done, ce_done, sc_done = sem("z_t"), sem("ebc_done"), sem("exp_done"), sem("ce_done"), sem("sc_done")
        turned, cb_read, xtok_done, xdec_done, state_mm, state_done = (sem("turned"), sem("cb_read"), sem("xtok_done"),
                                                                       sem("xdec_done"), sem("state_mm"), sem("state_done"))
        y_mm, y_read, ysq_done, gstat_mm, gvar_done, grinv_done = (sem("y_mm"), sem("y_read"), sem("ysq_done"),
                                                                   sem("gstat_mm"), sem("gvar_done"), sem("grinv_done"))
        yn_done, yn_hi, yn_lo = sem("yn_done"), sem("yn_hi"), sem("yn_lo")
        out_ready, out_done = sem("out_ready"), [sem("out_done0"), sem("out_done1")]

        phases = phase_table()
        if STOP is not None:
            phases = phases[:STOP]
        last_piece = phases[-1]["piece0"] + phases[-1]["iters"] * len(phases[-1]["widths"])

        def at(expr, n=1):
            return bass.ds(expr, n)

        def steps(engine, ph, body, chain, per):
            chain.close()
            body(0, True)
            chain.close()
            with engine.Fori(1, ph["iters"] - 1) as it:
                chain.begin(it - 1, per)
                body(it, False)
            chain.begin(ph["iters"] - 2, per)
            body(ph["iters"] - 1, False)
            chain.close(ph["iters"] - 1)

        def width_of(index, ph, q, last):
            w = ph["widths"]
            if q + LEAD < len(w):
                return w[q + LEAD]
            if not last:
                return w[q + LEAD - len(w)]
            return phases[index + 1]["widths"][q + LEAD - len(w)] if index + 1 < len(phases) else 0

        def norm_of(ph):
            return {("A1", 0): 0, ("F1", 0): 1, ("PL", 0): 2, ("B1", 1): 3, ("F1", 1): 4, ("PL", 1): 5}[
                (ph["name"], ph["layer"])] if ph["name"] in ("A1", "F1", "PL", "B1") and ph["half"] == 0 else None

        def next_norm(ph):
            return {("A2", 0, 0): 1, ("F2", 0, 1): 2, ("PL", 0, 0): 3, ("B2", 1, 1): 4, ("F2", 1, 1): 5,
                    ("PL", 1, 0): 6}.get((ph["name"], ph["layer"], ph["half"]))

        u_buf = {("A1", 0): 0, ("F1", 0): 0, ("PL", 0): 0, ("B1", 1): 1, ("F1", 1): 1, ("PL", 1): 1}

        def source(ph):
            name, layer = ph["name"], ph["layer"]
            if name == "A2":
                return 1
            if name == "B2":
                return 0
            if name == "F2":
                return 1 - u_buf[("F1", layer)]
            return u_buf[(name, layer)]

        def sumsq_base(norm):
            return norm * (KT + 1) - (KT // 2 if norm else 0)

        def next_u(norm):
            return {1: 0, 2: 0, 3: 1, 4: 1, 5: 1}[norm]

        block = ctx.enter_context(nc.Block())

        @block.sync
        def _(sp):
            sp.dma_start(gains[:], t["gains"]).then_inc(gains_in, 16)
            for c in range(4):
                sp.dma_start(h[:, 4 * c:4 * c + 4, :], t["xT"][:, 4 * c:4 * c + 4, :]).then_inc(x_in[c], 16)
            for index, ph in enumerate(phases):
                src, widths, n = t[ph["name"] + str(ph["layer"])], ph["widths"], len(ph["widths"])
                src0 = ph["half"] * ph["iters"]

                def body(it, first, ph=ph, src=src, widths=widths, n=n, src0=src0, index=index):
                    at0 = 0
                    for q, w in enumerate(widths):
                        p = it * n + ph["piece0"] + q
                        if index or q >= RING or not first:
                            sp.wait_ge(w_lo, p - RING + 1)
                        sp.dma_start(wraw[:, q % RING, 0:w * BLOCK],
                                     src[at(it + src0), at0:at0 + P * w * BLOCK].rearrange("o (p c) -> (o p) c", p=P)
                                     ).then_inc(w_landed[q % RING], 16)
                        at0 += P * w * BLOCK
                        if index == 0 and first and q == 1:
                            for dst, part in ((apar, "apar"), (bpar, "bpar"), (hpar, "hpar")):
                                sp.dma_start(dst[:], t[part]).then_inc(params_in, 16)
                        if ph["name"] == "A1" and q % 8 == 2:
                            head = it * 2 + q // 8
                            if not (first and q == 2):
                                sp.wait_ge(g_lo, head)
                            sp.dma_start(graw[:, 0:1024], t["gates"][at(head)].rearrange("o p c -> (o p) c")
                                         ).then_inc(g_landed, 16)
                        if ph["name"] == "B1" and q == 10:
                            group = it + ph["half"] * 4
                            if first and ph["half"] == 0:
                                sp.wait_ge(cs_out, 16)
                            else:
                                sp.wait_ge(y_mm, group * 2)
                            sp.dma_start(csb, cs_dram[at(group * GROUP_HEADS, GROUP_HEADS), :]
                                         .rearrange("e t -> (e t)").rearrange("(o n) -> o n", o=1)
                                         .broadcast_to([P, GROUP_HEADS * SEQ]).rearrange("p (e t) -> p e t", e=GROUP_HEADS)
                                         ).then_inc(cs_in, 16)
                if ph["name"] == "F2" and ph["half"] == 1:
                    if ph["layer"] == 1:
                        sp.wait_ge(p_lo, 1)
                    sp.dma_start(praw, t["pT"][ph["layer"]]).then_inc(p_in, 16)
                if ph["name"] == "F2" and ph["half"] == 1 and ph["layer"] == 0:
                    sp.wait_ge(g_lo, LRU_HEADS)
                    sp.dma_start(graw, t["dtw"]).then_inc(g_landed, 16)
                body(0, True)
                with sp.Fori(1, ph["iters"]) as it:
                    body(it, False)
            if STOP is None:
                for m in range(KT):
                    sp.wait_ge(out_ready, m + 1)
                    sp.dma_start(out[:, m, :], h[:, m, :]).then_inc(out_done[m % 2], 16)
                for s in out_done:
                    sp.wait_ge(s, 16 * KT // 2)
            else:
                sp.wait_ge(bank_free, 4 + phases[-1]["group0"] + phases[-1]["groups"] * phases[-1]["iters"])
                sp.wait_ge(h_done, 16 * sum(p["name"] == "PL" for p in phases))if any(p["name"] == "PL" for p in phases) else None
                sp.dma_start(out, h[:]).then_inc(out_done[0], 16)
                sp.wait_ge(out_done[0], 16)

        @block.tensor
        def _(pe):
            def three(dst, hi_w, lo_w, hi_x, lo_x, first, last):
                nc.tensor.matmul(dst, hi_w, hi_x, start=first, stop=False)
                nc.tensor.matmul(dst, hi_w, lo_x, start=False, stop=False)
                return nc.tensor.matmul(dst, lo_w, hi_x, start=False, stop=last)

            def piece(ph, it, q, blocks):
                p = it * len(ph["widths"]) + ph["piece0"] + q
                pe.wait_ge(w_lo, p + 1)
                for b, (before, dst, src, k, first, last) in enumerate(blocks):
                    for s, v in before:
                        pe.wait_ge(s, v)
                    cols = slice(b * BLOCK, (b + 1) * BLOCK)
                    mm = three(dst, whi[:, q % RING, cols], wlo[:, q % RING, cols], src[:, 0, k, :], src[:, 1, k, :],
                               first, last)
                mm.then_inc(w_used, 1)

            def free(ph, it, j):
                n = it * ph["groups"] + ph["group0"] + j
                return (bank_free, n + (1 if ph["name"] != "B1" else 3))

            def matmul_groups(ph, it, operand_ready):
                src, name = R[source(ph)], ph["name"]
                kts = {"F2": HALF}.get(name, KT)
                banks = BANKS2 if name == "B1" else BANKS4
                items = []
                for j in range(ph["groups"]):
                    if name == "PL" and j % 2:
                        for k in range(2):
                            items.append(([free(ph, it, j)] + [(p_lo, ph["layer"] + 1)] if k == 0 else [],
                                          bank[banks[j % 4]][:, 0:SEQ], src, 20 + k, k == 0, k == 1))
                        continue
                    for k in range(kts):
                        before = [free(ph, it, j)] if k == 0 else []
                        if j == 0:
                            before += operand_ready(k)
                        items.append((before, bank[banks[j % len(banks)]][:, 0:SEQ], src, k, k == 0, k == kts - 1))
                return items

            pe.wait_ge(const_done, 3)
            mids = 0
            ys = 0
            for index, ph in enumerate(phases):
                name, norm = ph["name"], norm_of(ph)
                if name in ("A1", "F1", "PL", "B1"):
                    number = {("A1", 0): 0, ("F1", 0): 1, ("PL", 0): 2, ("B1", 1): 3, ("F1", 1): 4, ("PL", 1): 5}[
                        (name, ph["layer"])]
                    base, tiles, ready = 16 * number, KT, u_ready
                elif name == "A2":
                    base, tiles, ready = 0, KT, y_lo
                elif name == "B2":
                    base, tiles, ready = 16 * ph["half"], KT, yn_lo
                else:
                    base, tiles, ready = mids, HALF, mid_ready
                    mids += HALF

                def operand_ready(k, base=base, tiles=tiles, ready=ready):
                    if k == 0:
                        return [(ready, base + tiles - 4)]
                    return [(ready, base + k + 1)] if k >= tiles - 4 else []

                def decay_products(base=base):
                    pe.wait_ge(g_lo, LRU_HEADS + 1)
                    for k in range(KT):
                        wr = R[1] if k < 8 else R[0]
                        c = slice((k % 8) * 128 % 256, (k % 8) * 128 % 256 + 128)
                        tile = 16 + (k % 8) // 2
                        mm = three(bank[7][:, 0:SEQ], wr[:, 0, tile, c], wr[:, 1, tile, c], R[1][:, 0, k, :],
                                   R[1][:, 1, k, :], k == 0, k == KT - 1)
                    mm.then_inc(dt_mm, 1)

                def decay_columns():
                    pe.wait_ge(wdec_done, 1)
                    for c in range(2):
                        nc.tensor.transpose(bank[5][:, c * 64:c * 64 + 64], dt_cs[:, c * CHUNK:(c + 1) * CHUNK],
                                            ident[0:HEADS, 0:HEADS])
                        nc.tensor.transpose(bank[5][:, 128 + c * 64:192 + c * 64], dt_v[:, c * CHUNK:(c + 1) * CHUNK],
                                            ident[0:HEADS, 0:HEADS])
                    nc.tensor.transpose(bank[5][:, 256:320], dt_dec, ident[0:HEADS, 0:HEADS]).then_inc(col_t, 1)

                def body(it, first, ph=ph, name=name, norm=norm, operand_ready=operand_ready):
                    items = matmul_groups(ph, it, operand_ready)
                    done = 0
                    for q, w in enumerate(ph["widths"]):
                        piece(ph, it, q, items[done:done + w])
                        done += w
                        if norm is not None and first and q == (2 if norm == 0 else 1):
                            pe.wait_ge(sumsq_done, sumsq_base(norm + 1))
                            if norm == 0:
                                pe.wait_ge(sumsq2_done, 1)
                                nc.tensor.matmul(bank[6][:, 0:SEQ], ones[:], sumsq2, start=True, stop=False)
                            nc.tensor.matmul(bank[6][:, 0:SEQ], ones[:], sumsq[:], start=norm != 0, stop=True
                                             ).then_inc(stats_done, 1)
                        if name == "B1" and ph["half"] == 0 and first:
                            if q == 2:
                                decay_products()
                            if q == 9:
                                decay_columns()
                        if name == "A1" and q % 8 == 7:
                            head = it * 2 + q // 8
                            pe.wait_ge(g_lo, head + 1)
                            pe.wait_ge(xc_lo, head * 2 + 2)
                            if not (first and q == 7):
                                pe.wait_ge(gate_t, head * 4)
                            b = 0
                            for g in range(2):
                                for m in range(2):
                                    for k in range(2):
                                        tile, c = 16 + b // 2, slice((b % 2) * 128, (b % 2) * 128 + 128)
                                        mm = three(bank[4 + g][:, m * SEQ:(m + 1) * SEQ], R[1][:, 0, tile, c],
                                                   R[1][:, 1, tile, c], R[1][:, 0, 20 + k, :], R[1][:, 1, 20 + k, :],
                                                   k == 0, k == 1)
                                        b += 1
                            mm.then_inc(g_used, 1)
                        if name == "B1":
                            group = it + ph["half"] * 4
                            if q == 3 and not first:
                                group_stats(group - 1)
                            if q == 13:
                                pe.wait_ge(silu_done, group * 6 + 6)
                                if not (first and ph["half"] == 0):
                                    pe.wait_ge(y_read, group * 4)
                                for c in range(2):
                                    nc.tensor.matmul(bank[4][:, c * CHUNK:(c + 1) * CHUNK],
                                                     ca[:, 0, c * CHUNK:(c + 1) * CHUNK],
                                                     ca[:, 1, c * CHUNK:(c + 1) * CHUNK], start=True, stop=True)
                                nc.tensor.transpose(bank[4][:, 256:384], ca[:, 0, 0:CHUNK], ident[:])
                                for c in range(2):
                                    for j in range(4):
                                        mm = nc.tensor.transpose(bank[5 + c][:, j * P:(j + 1) * P],
                                                                 ca[:, 2 + j, c * CHUNK:(c + 1) * CHUNK], ident[:])
                                mm.then_inc(turned, 1)
                            if q == 15:
                                pe.wait_ge(xdec_done, group + 1)
                                nc.tensor.matmul(bank[5][:, 0:512], btok, xdec, start=True, stop=True
                                                 ).then_inc(state_mm, 1)
                            if q in (17, 19):
                                pair0 = 0 if q == 17 else 2
                                pe.wait_ge(sc_done, group * 2 + q // 2 - 7)
                                if q == 17:
                                    pe.wait_ge(ce_done, group + 1)
                                    pe.wait_ge(state_done, group + 1)
                                for j in range(pair0, pair0 + 2):
                                    dst = bank[6 if j < 2 else 4]
                                    for e in range(2):
                                        head, rows = 2 * j + e, slice(64 * e, 64 * e + 64)
                                        cols = (j % 2) * SEQ
                                        ch = slice(head * 64, head * 64 + 64)
                                        nc.tensor.matmul(dst[rows, cols:cols + CHUNK], xtok[:, 0, ch],
                                                         csb[:, head, 0:CHUNK], start=True, stop=True)
                                        nc.tensor.matmul(dst[rows, cols + CHUNK:cols + SEQ], xtok[:, 1, ch],
                                                         csb[:, head, CHUNK:SEQ], start=True, stop=False)
                                        mm = nc.tensor.matmul(dst[rows, cols + CHUNK:cols + SEQ], state[:, ch],
                                                              ebc[:, head, :], start=False, stop=True)
                                mm.then_inc(y_mm, 1)

                def group_stats(group):
                    for j in range(4):
                        pe.wait_ge(ysq_done, group * 4 + j + 1)
                        mm = nc.tensor.matmul(bank[7][:, 0:SEQ], ones[:], ysq[:, j, :], start=j == 0, stop=j == 3)
                    mm.then_inc(gstat_mm, 1)

                body(0, True)
                with pe.Fori(1, ph["iters"]) as it:
                    body(it, False)
                if name == "B1":
                    group_stats(ph["half"] * 4 + 3)
            if STOP is None:
                pe.wait_ge(sumsq_done, sumsq_base(7))
                nc.tensor.matmul(bank[6][:, 0:SEQ], ones[:], sumsq[:], start=True, stop=True).then_inc(stats_done, 1)

        @block.scalar
        def _(act):
            own = Chain(act, act_own)

            def hi(ph_piece, q, w, early=False):
                slot = q % RING
                act.wait_ge(w_landed[slot], (ph_piece - slot) * (16 // RING) + 16)
                if not early:
                    act.wait_ge(w_used, ph_piece - RING + 1)
                nc.scalar.activation(whi[:, slot, 0:w * BLOCK], wraw[:, slot, 0:w * BLOCK], ACT.Copy).then_inc(w_hi, 1)

            def softexp(n, dst, src):
                act.wait_ge(softexp_in, n)
                nc.scalar.activation(dst, src, ACT.Exp).then_inc(softexp_out, 1)

            def norm(k):
                act.wait_ge(var_done, k + 1)
                nc.scalar.activation(rinv[:], rinvh[:], ACT.Sqrt).then_inc(rinv_done, 1)

            for q in range(LEAD):
                hi(q, q, 8, early=True)
                if q < 2:
                    act.wait_ge(gains_in, 16)
                    act.wait_ge(x_in[2 * q], 16)
                    act.wait_ge(x_in[2 * q + 1], 16)
                    for m in range(8 * q, 8 * q + 8):
                        nc.scalar.activation(R[0][:, 0, m, :], h[:, m, :], ACT.Copy, scale=gains[:, m:m + 1]
                                             ).then_inc(u0_hi, 1)
            softexp(1, kt_b, kt_a)
            act.wait_ge(kk_done, 2)
            for index, ph in enumerate(phases):
                name, n = ph["name"], len(ph["widths"])
                if name == "PL":
                    src = R[u_buf[("PL", ph["layer"])]]
                    act.wait_ge(p_in, 16 * (ph["layer"] + 1))
                    nc.scalar.activation(src[:, 0, 20:22, :], praw.rearrange("p (k t) -> p k t", k=2), ACT.Copy
                                         ).then_inc(p_hi, 1)

                def decay_steps(q):
                    if q == 3:
                        softexp(2, dt_e, dt_w)
                        nc.scalar.activation(hpar[:, 1:2], hpar[:, 1:2], ACT.Exp).then_inc(a_exp, 1)
                    elif q == 7:
                        act.wait_ge(cs_done, 1)
                        act.dma_start(cs_dram, dt_cs).then_inc(cs_out, 16)
                        nc.scalar.activation(dt_dec, dt_cs[:, 0:CHUNK], ACT.Exp, bias=dt_cs[:, CHUNK - 1:CHUNK],
                                             scale=-1.0).then_inc(dec_exp, 1)

                def split_dt_weights():
                    act.wait_ge(g_landed, 16 * (LRU_HEADS + 1))
                    for r, lo in ((1, 0), (0, 1024)):
                        last = nc.scalar.activation(R[r][:, 0, 16:20, :],
                                                    graw[:, lo:lo + 1024].rearrange("p (k t) -> p k t", k=4), ACT.Copy)
                    last.then_inc(g_hi, 1)

                def gates(head):
                    act.wait_ge(g_used, head + 1)
                    for g, dst in ((0, tr), (1, ti)):
                        for j in range(2):
                            nc.scalar.activation(dst[:, j, :], bank[4 + g][:, j * SEQ:(j + 1) * SEQ], ACT.Tanh,
                                                 bias=apar[:, at(head * 2 + j), 5 + g:6 + g].rearrange("p a b -> p (a b)"),
                                                 scale=0.5).then_inc(gate_t, 1)

                def decays(head):
                    act.wait_ge(gate_t, head * 4 + 2)
                    kk = [apar[:, at(head * 2 + j), 7:8].rearrange("p a b -> p (a b)") for j in range(2)]
                    for j in range(2):
                        nc.scalar.activation(av[:, j, :], tr[:, j, :], ACT.Exp, bias=kk[j], scale=kk[j]).then_inc(a_done, 1)
                    for j in range(2):
                        nc.scalar.activation(tr[:, j, :], tr[:, j, :], ACT.Tanh, bias=kk[j], scale=kk[j]).then_inc(e_done, 1)

                def mult(head):
                    act.wait_ge(s_done, head + 1)
                    nc.scalar.activation(sq, sq, ACT.Sqrt, scale=-1.0).then_inc(mult_done, 1)

                def gelu(head, hh):
                    act.wait_ge(gelu_q, head + 1)
                    nc.scalar.activation(ge, ge, ACT.Tanh, scale=GELU_C).then_inc(gelu_t, 1)

                def lru_y(head, hh):
                    act.wait_ge(y_done, head + 1)
                    nc.scalar.activation(R[1][:, 0, at(head * 2, 2), :], yv[:, hh], ACT.Copy).then_inc(y_hi, 1)

                def chain_step(head, hh, s):
                    if s == 0:
                        gates(head)
                    elif s == 1:
                        decays(head)
                    elif s == 2:
                        gelu(head, hh)
                    elif s == 4:
                        mult(head)
                    elif s == 6:
                        lru_y(head, hh)

                def body(it, first, ph=ph, name=name, n=n, index=index):
                    last = isinstance(it, int) and it == ph["iters"] - 1
                    for q in range(n):
                        p = it * n + ph["piece0"] + q
                        w = width_of(index, ph, q, last)
                        if w:
                            hi(p + LEAD, q + LEAD, w, early=first and index == 0 and q == 0)
                        if norm_of(ph) is not None and first and q == 1:
                            norm(norm_of(ph))
                        if name == "PL" and ph["layer"] == 0 and first and q == 5:
                            split_dt_weights()
                        if name == "A1":
                            head, hh, s = it * 2 + q // 8, q // 8, q % 8
                            if not (first and q < 8):
                                chain_step(head - 1, 1 - hh, s)
                            if s in (3, 5):
                                j = (s - 3) // 2
                                act.wait_ge(xc_done, head * 2 + j + 1)
                                if not (first and q < 8):
                                    act.wait_ge(g_used, head)
                                nc.scalar.activation(R[1][:, 0, 20 + j, :], xc[:, hh, j, :], ACT.Copy).then_inc(xc_hi, 1)
                            if s == 5:
                                act.wait_ge(g_landed, head * 16 + 16)
                                if not (first and q < 8):
                                    act.wait_ge(g_used, head)
                                nc.scalar.activation(R[1][:, 0, 16:20, :],
                                                     graw[:, 0:1024].rearrange("p (k t) -> p k t", k=4), ACT.Copy
                                                     ).then_inc(g_hi, 1)
                        if name == "F1":
                            f = it * 2 + ph["layer"] * FF_TILES + ph["half"] * HALF
                            g = it * 4 + ph["group0"] + 4
                            if q in (1, 5):
                                j = q // 4
                                act.wait_ge(bank_free, g + 2 * j + 1)
                                nc.scalar.activation(swi_t[:, j, :], swi_g[:, j, :], ACT.Tanh).then_inc(tanh_done, 1)
                            if q in (3, 7):
                                j = q // 4
                                act.wait_ge(mid_done, f + j + 1)
                                nc.scalar.activation(R[1 - source(ph)][:, 0, at(it * 2 + j), :].rearrange("p a t -> p (a t)"),
                                                     swi_u[:, j, :], ACT.Copy).then_inc(mid_hi, 1)
                        if name == "PL" and q in (3, 7):
                            j = q // 4
                            g = it * 4 + ph["group0"] + 4
                            act.wait_ge(bank_free, g + 2 * j + 1)
                            nc.scalar.activation(swi_t[:, j, :], swi_g[:, j, :], ACT.Tanh).then_inc(ple_t, 1)
                        if name == "B1":
                            group = it + ph["half"] * 4
                            very_first = first and ph["half"] == 0
                            if very_first:
                                decay_steps(q)
                            if q == 0 and not first:
                                z_tanh(it, 19, group - 1)
                            if q == 5 and not first:
                                group_rinv(group - 1)
                            if q == 7 and not first:
                                group_hi(group - 1, it - 1)
                            if q % 2 == 0 and 2 <= q <= 12:
                                nt = q // 2 - 1
                                act.wait_ge(conv_done, group * 6 + nt + 1)
                                nc.scalar.activation(cth[:, nt % 2, :], ca[:, nt, :], ACT.Tanh).then_inc(conv_t, 1)
                            if q in (14, 16, 18):
                                z_tanh(it, q - 1, group)
                            if q == 9:
                                act.wait_ge(cs_in, group * 16 + 16)
                                if not very_first:
                                    act.wait_ge(y_mm, group * 2)
                                nc.scalar.activation(ebc, csb[:, :, CHUNK:SEQ], ACT.Exp).then_inc(ebc_done, 1)
                            if q in (10, 11, 12, 13):
                                if q == 10:
                                    if very_first:
                                        act.wait_ge(col_done, 1)
                                    act.wait_ge(ebc_done, group + 1)
                                e0 = 2 * (q - 10)
                                for e in (e0, e0 + 1):
                                    for c in range(2):
                                        r = nc.scalar.activation(csb[:, e, c * CHUNK:(c + 1) * CHUNK],
                                                                 csb[:, e, c * CHUNK:(c + 1) * CHUNK], ACT.Relu,
                                                                 bias=cst[:, c, at(group * GROUP_HEADS + e)], scale=-1.0)
                                own.link(r)
                                nc.scalar.activation(csb[:, e0:e0 + 2, :], csb[:, e0:e0 + 2, :], ACT.Exp, scale=-1.0
                                                     ).then_inc(exp_done, 1)
                            if q == 14:
                                act.wait_ge(turned, group + 1)
                                for c in range(2):
                                    nc.scalar.activation(xtok[:, c, :], bank[5 + c][:], ACT.Copy).then_inc(xtok_done, 1)
                            if q == 16:
                                act.wait_ge(state_mm, group + 1)
                                nc.scalar.activation(state, bank[5][:], ACT.Copy).then_inc(state_done, 1)

                def z_tanh(it, q, group):
                    j = q // 2 - 6
                    act.wait_ge(bank_free, (it - (j == 3)) * 10 + ph["group0"] + 4 + q // 2 + 1)
                    nc.scalar.activation(cth[:, j % 2, :], zt[:, j, :], ACT.Tanh).then_inc(z_t, 1)

                def group_rinv(group):
                    act.wait_ge(gvar_done, group + 1)
                    nc.scalar.activation(grms[:], grms[:], ACT.Sqrt).then_inc(grinv_done, 1)

                def group_hi(group, local):
                    local = local * 4
                    for j in range(4):
                        act.wait_ge(yn_done, group * 4 + j + 1)
                        nc.scalar.activation(R[0][:, 0, at(local + j), :].rearrange("p a t -> p (a t)"), zt[:, j, :], ACT.Copy
                                             ).then_inc(yn_hi, 1)

                steps(act, ph, body, own, 4 if name == "B1" else 0)
                if name == "A1":
                    for s in range(8):
                        chain_step(LRU_HEADS - 1, 1, s)
                if name == "B1":
                    z_tanh(4, 19, ph["half"] * 4 + 3)
                    group_rinv(ph["half"] * 4 + 3)
                    group_hi(ph["half"] * 4 + 3, 3)
            if STOP is None:
                norm(6)

        @block.vector
        def _(dve):
            own = Chain(dve, dve_own)
            V = nc.vector

            def lo(p, q, w):
                slot = q % RING
                dve.wait_ge(w_hi, p + 1)
                V.tensor_tensor(wlo[:, slot, 0:w * BLOCK], wraw[:, slot, 0:w * BLOCK],
                                whi[:, slot, 0:w * BLOCK].bitcast(F32), ALU.subtract).then_inc(w_lo, 1)

            def softplus_parts(n, x, e_in, e, w, z, r):
                softplus_head(x, e_in)
                softplus_mid(n, e, w, z, r)
                softplus_tail(x, w, z, r)

            def softplus_head(x, e_in):
                own.link(V.tensor_scalar(e_in, x, -1.0, None, ALU.mult))
                V.tensor_tensor(e_in, e_in, x, ALU.min).then_inc(softexp_in, 1)

            def softplus_mid(n, e, w, z, r):
                dve.wait_ge(softexp_out, n)
                own.link(V.tensor_scalar(z, e, 2.0, None, ALU.add))
                own.link(V.reciprocal(r, z))
                own.link(V.tensor_tensor(w, e, r, ALU.mult))
                own.link(V.tensor_tensor(z, w, w, ALU.mult))

            def softplus_tail(x, w, z, r):
                own.link(V.tensor_scalar(r, z, 1.0 / 17, None, ALU.mult))
                for c in (15, 13, 11, 9, 7, 5, 3):
                    own.link(V.scalar_tensor_tensor(out=r, in0=r, scalar=1.0 / c, in1=z, op0=ALU.add, op1=ALU.mult))
                own.link(V.scalar_tensor_tensor(out=r, in0=r, scalar=1.0, in1=w, op0=ALU.add, op1=ALU.mult))
                own.link(V.tensor_scalar(x, x, 0.0, None, ALU.max))
                own.link(V.scalar_tensor_tensor(out=x, in0=r, scalar=2.0, in1=x, op0=ALU.mult, op1=ALU.add))

            def u_split(norm, m, count, buf):
                g = gains[:, at(m + norm * KT)]
                dst = R[buf]
                def tile(x):
                    return x.rearrange("p a t -> p (a t)")
                V.tensor_scalar(tile(dst[:, 0, at(m), :]), tile(h[:, at(m), :]), g, None, ALU.mult).then_inc(uh_done, 1)
                dve.wait_ge(uh_done, count)
                V.scalar_tensor_tensor(out=tile(dst[:, 1, at(m), :]), in0=tile(h[:, at(m), :]), scalar=g,
                                       in1=tile(dst[:, 0, at(m), :]).bitcast(F32), op0=ALU.mult, op1=ALU.subtract
                                       ).then_inc(u_ready, 1)

            def norm(k):
                dve.wait_ge(stats_done, k + 1)
                own.link(V.tensor_scalar(rinvh[:], bank[6][:, 0:SEQ], 1.0 / D, EPS, ALU.mult, ALU.add))
                V.reciprocal(rinvh[:], rinvh[:]).then_inc(var_done, 1)
                dve.wait_ge(rinv_done, k + 1)
                own.link(V.tensor_scalar(rinvh[:], rinv[:], 0.5, None, ALU.mult))

            for _ in range(4):
                dve.sem_inc(bank_free, 1)
            own.mark(V.memset(xpad, 0.0))
            dve.wait_ge(gains_in, 16)
            for q in range(LEAD):
                lo(q, q, 8)
                if q < 2:
                    for m in range(8 * q, 8 * q + 8):
                        dve.wait_ge(u0_hi, m + 1)
                        V.scalar_tensor_tensor(out=R[0][:, 1, m, :], in0=h[:, m, :], scalar=gains[:, m:m + 1],
                                               in1=R[0][:, 0, m, :].bitcast(F32), op0=ALU.mult, op1=ALU.subtract
                                               ).then_inc(u_ready, 1)
            own.link(V.tensor_tensor(sumsq2, h[:, 8, :], h[:, 8, :], ALU.mult))
            for m in range(9, KT):
                own.link(V.tensor_tensor(square3, h[:, m, :], h[:, m, :], ALU.mult))
                last = V.tensor_tensor(sumsq2, sumsq2, square3, ALU.add)
                if m < KT - 1:
                    own.link(last)
            last.then_inc(sumsq2_done, 1)
            dve.wait_ge(params_in, 48)
            lam = apar[:, :, 7]
            own.link(V.tensor_scalar(kt_c, lam, -1.0, None, ALU.mult))
            kk_w, kk_z, kk_r = (sq[:, 0, 0:16], sq[:, 0, 16:32], sq[:, 0, 32:48])
            softplus_parts(1, kt_c, kt_a, kt_b, kk_w, kk_z, kk_r)
            V.tensor_scalar(lam, kt_c, -4.0, None, ALU.mult).then_inc(kk_done, 1)
            V.tensor_scalar(apar[:, :, 5:7], apar[:, :, 5:7], 0.5, None, ALU.mult).then_inc(kk_done, 1)
            own.link(V.tensor_scalar(bpar[:, :, 0:30], bpar[:, :, 0:30], 0.5, None, ALU.mult))
            own.close(1)

            for index, ph in enumerate(phases):
                name, n = ph["name"], len(ph["widths"])
                if name == "PL":
                    src = R[u_buf[("PL", ph["layer"])]]
                    dve.wait_ge(p_hi, ph["layer"] + 1)
                    V.tensor_tensor(src[:, 1, 20:22, :], praw.rearrange("p (k t) -> p k t", k=2),
                                    src[:, 0, 20:22, :].bitcast(F32), ALU.subtract).then_inc(p_lo, 1)
                if name == "B1" and ph["half"] == 0:
                    own.mark(V.memset(cpad, 0.0))
                    own.link(V.memset(dt_one, 1.0))
                    dve.wait_ge(const_done, 3)
                own.close(1)

                def split_dt_weights():
                    dve.wait_ge(g_hi, LRU_HEADS + 1)
                    for r, at0 in ((1, 0), (0, 1024)):
                        last = V.tensor_tensor(R[r][:, 1, 16:20, :],
                                               graw[:, at0:at0 + 1024].rearrange("p (k t) -> p k t", k=4),
                                               R[r][:, 0, 16:20, :].bitcast(F32), ALU.subtract)
                    last.then_inc(g_lo, 1)

                def decay_steps(q):
                    if q == 3:
                        dve.wait_ge(dt_mm, 1)
                        own.link(V.tensor_tensor(dt_x, bank[7][0:HEADS, 0:SEQ], rinv[0:HEADS, :], ALU.mult))
                        own.link(V.tensor_scalar(dt_v, dt_x, hpar[:, 0:1], None, ALU.add))
                        softplus_head(dt_v, dt_w)
                    elif q == 4:
                        softplus_mid(2, dt_e, dt_w, dt_z, dt_r)
                    elif q == 6:
                        softplus_tail(dt_v, dt_w, dt_z, dt_r)
                        dve.wait_ge(a_exp, 1)
                        own.link(V.tensor_scalar(dt_x, dt_v, hpar[:, 1:2], -1.0, ALU.mult, ALU.mult))
                        V.tensor_tensor_scan(dt_cs[:, 0:CHUNK], dt_one[:, 0:CHUNK], dt_x[:, 0:CHUNK], 0.0, ALU.mult, ALU.add
                                             ).then_inc(cs_done0, 1)
                        dve.wait_ge(cs_done0, 1)
                        V.tensor_tensor_scan(dt_cs[:, CHUNK:SEQ], dt_one[:, CHUNK:SEQ], dt_x[:, CHUNK:SEQ], 0.0,
                                             ALU.mult, ALU.add).then_inc(cs_done, 1)
                    elif q == 8:
                        dve.wait_ge(dec_exp, 1)
                        V.tensor_tensor(dt_dec, dt_dec, dt_v[:, 0:CHUNK], ALU.mult).then_inc(wdec_done, 1)
                    elif q == 10:
                        dve.wait_ge(col_t, 1)
                        V.tensor_copy(cst, bank[5][:, 0:128].rearrange("p (c e) -> p c e", c=2)).then_inc(col_done, 1)
                        own.mark(V.tensor_copy(dtt, bank[5][:, 128:256].rearrange("p (c e) -> p c e", c=2)))
                        own.link(V.tensor_copy(wdt, bank[5][:, 256:320]))

                def flat(x):
                    return x.rearrange("p a t -> p (a t)")

                def conv(pad, dst, taps, bias, count, done):
                    own.link(V.tensor_scalar(dst, pad[:, 3:3 + SEQ], taps(3), bias, ALU.mult, ALU.add))
                    for k in (2, 1):
                        own.link(V.scalar_tensor_tensor(out=dst, in0=pad[:, k:k + SEQ], scalar=taps(k), in1=dst,
                                                        op0=ALU.mult, op1=ALU.add))
                    V.scalar_tensor_tensor(out=dst, in0=pad[:, 0:SEQ], scalar=taps(0), in1=dst, op0=ALU.mult,
                                           op1=ALU.add).then_inc(done, 1)

                def chain_step(head, hh, s):
                    if s == 1:
                        dve.wait_ge(cube_done, head + 1)
                        V.scalar_tensor_tensor(out=ge, in0=ge, scalar=0.044715, in1=yv[:, hh], op0=ALU.mult, op1=ALU.add
                                               ).then_inc(gelu_q, 1)
                    elif s == 3:
                        dve.wait_ge(asq_done, head + 1)
                        dve.wait_ge(e_done, head * 2 + 2)
                        V.scalar_tensor_tensor(out=sq, in0=sq, scalar=1.0, in1=tr, op0=ALU.add, op1=ALU.mult
                                               ).then_inc(s_done, 1)
                        dve.wait_ge(gate_t, head * 4 + 4)
                        own.link(V.scalar_tensor_tensor(out=ti, in0=ti, scalar=1.0, in1=xc[:, hh], op0=ALU.add, op1=ALU.mult))
                        dve.wait_ge(gelu_t, head + 1)
                        own.link(V.scalar_tensor_tensor(out=ge, in0=ge, scalar=1.0, in1=yv[:, hh], op0=ALU.add, op1=ALU.mult))
                    elif s == 5:
                        dve.wait_ge(mult_done, head + 1)
                        own.link(V.tensor_tensor(ti, ti, sq, ALU.mult))
                        for j in range(2):
                            own.mark(V.tensor_tensor_scan(tr[:, j, :], av[:, j, :], ti[:, j, :], 0.0, ALU.mult, ALU.add))
                        own.need(own.latest())
                        V.scalar_tensor_tensor(out=yv[:, hh], in0=tr, scalar=0.25, in1=ge, op0=ALU.mult, op1=ALU.mult
                                               ).then_inc(y_done, 1)

                def body(it, first, ph=ph, name=name, n=n, index=index):
                    last = isinstance(it, int) and it == ph["iters"] - 1
                    for q in range(n):
                        p = it * n + ph["piece0"] + q
                        w = width_of(index, ph, q, last)
                        if w:
                            lo(p + LEAD, q + LEAD, w)
                        g0 = it * ph["groups"] + ph["group0"] + 4
                        if norm_of(ph) is not None and first and q == 1:
                            norm(norm_of(ph))
                        if name == "PL" and ph["layer"] == 0 and first and q == 6:
                            split_dt_weights()
                        if name == "A1":
                            head, hh, s = it * 2 + q // 8, q // 8, q % 8
                            if not (first and q < 8):
                                chain_step(head - 1, 1 - hh, s)
                            if s % 2:
                                dve.wait_ge(w_used, p + 1)
                                src = bank[BANKS4[s // 2]][:, 0:SEQ]
                            if s in (1, 3):
                                j = s // 2
                                tile = head * 2 + j
                                V.tensor_tensor(xpad[:, j, 3:3 + SEQ], src, rinv[:], ALU.mult).then_inc(bank_free, 1)
                                dve.wait_ge(bank_free, g0 + hh * 4 + j + 1)
                                conv(xpad[:, j], xc[:, hh, j, :],
                                     lambda k, tile=tile: flat(apar[:, at(tile), k:k + 1]), flat(apar[:, at(tile), 4:5]),
                                     tile, xc_done)
                            if s in (5, 7):
                                if s == 5 and not first:
                                    dve.wait_ge(y_lo, head * 2 - 2)
                                V.tensor_tensor(yv[:, hh, s // 2 - 2, :], src, rinv[:], ALU.mult).then_inc(bank_free, 1)
                            if s == 6:
                                dve.wait_ge(g_hi, head + 1)
                                V.tensor_tensor(R[1][:, 1, 16:20, :], graw[:, 0:1024].rearrange("p (k t) -> p k t", k=4),
                                                R[1][:, 0, 16:20, :].bitcast(F32), ALU.subtract).then_inc(g_lo, 1)
                        if name in ("A2", "F2", "B2"):
                            per = n // 4
                            if q % per == per - 1:
                                j = q // per
                                m = it * 4 + j
                                dve.wait_ge(w_used, p + 1)
                                V.tensor_tensor(flat(h[:, at(m), :]), bank[BANKS4[j]][:, 0:SEQ], flat(h[:, at(m), :]), ALU.add
                                                ).then_inc(bank_free, 1)
                                if next_norm(ph) is not None:
                                    dve.wait_ge(bank_free, g0 + j + 1)
                                    u_split(next_norm(ph), m, m + (next_norm(ph) - 1) * KT + 1, next_u(next_norm(ph)))
                        if name == "F1":
                            f = it * 2 + ph["layer"] * FF_TILES + ph["half"] * HALF
                            j = q // 4
                            if q in (1, 5):
                                dve.wait_ge(w_used, p + 1)
                                V.tensor_tensor(swi_g[:, j, :], bank[BANKS4[2 * j]][:, 0:SEQ], rinvh[:], ALU.mult
                                                ).then_inc(bank_free, 1)
                            if q in (2, 6):
                                dve.wait_ge(tanh_done, f + j + 1)
                                own.mark(V.scalar_tensor_tensor(out=swi_g[:, j, :], in0=swi_t[:, j, :], scalar=1.0,
                                                                in1=swi_g[:, j, :], op0=ALU.add, op1=ALU.mult))
                            if q in (3, 7):
                                dve.wait_ge(w_used, p + 1)
                                if not (first and ph["layer"] == 0 and ph["half"] == 0):
                                    dve.wait_ge(mid_ready, f + j - 1)
                                V.tensor_tensor(swi_u[:, j, :], bank[BANKS4[2 * j + 1]][:, 0:SEQ], rinv[:], ALU.mult
                                                ).then_inc(bank_free, 1)
                                dve.wait_ge(bank_free, g0 + 2 * j + 2)
                                own.need(own.latest())
                                V.tensor_tensor(swi_u[:, j, :], swi_g[:, j, :], swi_u[:, j, :], ALU.mult
                                                ).then_inc(mid_done, 1)
                        if name == "PL":
                            if q in (3, 7):
                                j = q // 4
                                dve.wait_ge(w_used, p + 1)
                                V.tensor_tensor(swi_g[:, j, :], bank[BANKS4[2 * j]][:, 0:SEQ], rinvh[:], ALU.mult
                                                ).then_inc(bank_free, 1)
                            if q in (4, 7):
                                j = 0 if q == 4 else 1
                                m = it * 2 + j
                                done = m + ph["layer"] * KT + 1
                                dve.wait_ge(ple_t, done)
                                V.scalar_tensor_tensor(out=swi_g[:, j, :], in0=swi_t[:, j, :], scalar=1.0,
                                                       in1=bank[BANKS4[2 * j + 1]][:, 0:SEQ], op0=ALU.add, op1=ALU.mult
                                                       ).then_inc(bank_free, 1)
                                dve.wait_ge(bank_free, g0 + 2 * j + 2)
                                V.scalar_tensor_tensor(out=flat(h[:, at(m), :]), in0=swi_g[:, j, :], scalar=0.5,
                                                       in1=flat(h[:, at(m), :]), op0=ALU.mult, op1=ALU.add
                                                       ).then_inc(h_done, 1)
                                if ph["layer"] == 0:
                                    dve.wait_ge(h_done, done)
                                    u_split(3, m, m + 2 * KT + 1, next_u(3))
                        if name == "B1":
                            group = it + ph["half"] * 4
                            very_first = first and ph["half"] == 0
                            if very_first:
                                decay_steps(q)
                            if q == 0 and not first:
                                z_silu(group - 1, 3)
                                group_y(group - 1)
                            if q == 4 and not first:
                                group_var(group - 1)
                            if q == 6 and not first:
                                group_norm(group - 1)
                            if q % 2 == 0 and 2 <= q <= 12:
                                nt = q // 2 - 1
                                dve.wait_ge(conv_t, group * 6 + nt + 1)
                                V.scalar_tensor_tensor(out=ca[:, nt, :], in0=cth[:, nt % 2, :], scalar=1.0,
                                                       in1=ca[:, nt, :], op0=ALU.add, op1=ALU.mult).then_inc(silu_done, 1)
                            if q % 2 == 1:
                                dve.wait_ge(w_used, p + 1)
                                src = bank[BANKS2[q // 2 % 2]][:, 0:SEQ]
                            if q % 2 == 1 and q < 12:
                                nt = q // 2
                                par = lambda k, nt=nt, group=group: flat(bpar[:, at(group), nt * 5 + k:nt * 5 + k + 1])
                                V.tensor_tensor(cpad[:, nt % 2, 3:3 + SEQ], src, rinv[:], ALU.mult).then_inc(bank_free, 1)
                                dve.wait_ge(bank_free, g0 + nt + 1)
                                conv(cpad[:, nt % 2], ca[:, nt, :], par, par(4), None, conv_done)
                            if q % 2 == 1 and q > 12:
                                j = q // 2 - 6
                                if j == 0 and not very_first:
                                    dve.wait_ge(yn_lo, group * 4)
                                V.tensor_tensor(zt[:, j, :], src, rinvh[:], ALU.mult).then_inc(bank_free, 1)
                            if q in (14, 16, 18):
                                z_silu(group, q // 2 - 7)
                            if q == 14:
                                dve.wait_ge(turned, group + 1)
                                own.mark(V.tensor_tensor(cbm, bank[4][:, 0:256].rearrange("p (c l) -> p c l", c=2),
                                                         causal[:].rearrange("p (c l) -> p c l", c=1)
                                                         .broadcast_to([P, 2, CHUNK]), ALU.mult))
                                own.link(V.tensor_copy(btok, bank[4][:, 256:384]))
                                dve.wait_ge(xtok_done, group * 2 + 1)
                                V.tensor_tensor(xdec.rearrange("p (e c) -> p e c", e=GROUP_HEADS),
                                                xtok[:, 0, :].rearrange("p (e c) -> p e c", e=GROUP_HEADS),
                                                wdt[:, at(group * GROUP_HEADS, GROUP_HEADS)]
                                                .rearrange("p (e c) -> p e c", c=1).broadcast_to([P, GROUP_HEADS, 64]),
                                                ALU.mult).then_inc(xdec_done, 1)
                            if q in (15, 17):
                                h0 = 0 if q == 15 else 4
                                dve.wait_ge(exp_done, group * 4 + h0 // 2 + 2)
                                if q == 15:
                                    own.need(own.latest())
                                for e in range(h0, h0 + 4):
                                    for c in range(2):
                                        s = V.scalar_tensor_tensor(
                                            out=csb[:, e, c * CHUNK:(c + 1) * CHUNK], in0=csb[:, e, c * CHUNK:(c + 1) * CHUNK],
                                            scalar=dtt[:, c, at(group * GROUP_HEADS + e)], in1=cbm[:, c, :],
                                            op0=ALU.mult, op1=ALU.mult)
                                s.then_inc(sc_done, 1)

                def z_silu(group, j):
                    dve.wait_ge(z_t, group * 4 + j + 1)
                    own.mark(V.scalar_tensor_tensor(out=zt[:, j, :], in0=cth[:, j % 2, :], scalar=1.0,
                                                    in1=zt[:, j, :], op0=ALU.add, op1=ALU.mult))

                def group_y(group):
                    dsk = lambda j: flat(bpar[:, at(group), 30 + j:31 + j])
                    dve.wait_ge(y_mm, group * 2 + 2)
                    own.need(own.latest())
                    for j in range(4):
                        src = bank[6 if j < 2 else 4][:, (j % 2) * SEQ:(j % 2 + 1) * SEQ]
                        V.scalar_tensor_tensor(out=ca[:, 2 + j, :], in0=ca[:, 2 + j, :], scalar=dsk(j), in1=src,
                                               op0=ALU.mult, op1=ALU.add).then_inc(y_read, 1)
                    for j in range(4):
                        dve.wait_ge(y_read, group * 4 + j + 1)
                        V.tensor_tensor(zt[:, j, :], ca[:, 2 + j, :], zt[:, j, :], ALU.mult).then_inc(yz_done, 1)

                def group_var(group):
                    dve.wait_ge(gstat_mm, group + 1)
                    own.link(V.tensor_scalar(grms[:], bank[7][:, 0:SEQ], 1.0 / 512, EPS, ALU.mult, ALU.add))
                    V.reciprocal(grms[:], grms[:]).then_inc(gvar_done, 1)

                def group_norm(group):
                    dve.wait_ge(grinv_done, group + 1)
                    for j in range(4):
                        V.scalar_tensor_tensor(out=zt[:, j, :], in0=zt[:, j, :], scalar=flat(bpar[:, at(group), 34 + j:35 + j]),
                                               in1=grms[:], op0=ALU.mult, op1=ALU.mult).then_inc(yn_done, 1)

                steps(dve, ph, body, own, {"A1": 22, "B1": 25, "F1": 2}.get(name, 0))
                if name == "A1":
                    for s in range(8):
                        chain_step(LRU_HEADS - 1, 1, s)
                if name == "B1":
                    z_silu(ph["half"] * 4 + 3, 3)
                    group_y(ph["half"] * 4 + 3)
                    group_var(ph["half"] * 4 + 3)
                    group_norm(ph["half"] * 4 + 3)
                own.close()
            if STOP is None:
                norm(6)
                for m in range(KT):
                    V.scalar_tensor_tensor(out=h[:, m, :], in0=h[:, m, :], scalar=gains[:, 6 * KT + m:6 * KT + m + 1],
                                           in1=rinv[:], op0=ALU.mult, op1=ALU.mult).then_inc(out_ready, 1)

        @block.gpsimd
        def _(pool):
            G = nc.gpsimd
            own = Chain(pool, pool_own)
            G.memset(ones[:], 1.0).then_inc(const_done, 1)
            own.link(G.memset(ident[:], 0.0))
            own.link(G.memset(causal[:], 1.0))
            G.affine_select(out=ident[:], in_=ident[:], compare_op=ALU.not_equal, fill=1.0, base=0,
                            pattern=[[-1, P]], channel_multiplier=1).then_inc(const_done, 1)
            G.affine_select(out=causal[:], in_=causal[:], compare_op=ALU.is_ge, fill=0.0, base=0,
                            pattern=[[1, CHUNK]], channel_multiplier=-1).then_inc(const_done, 1)
            own.close(1)

            def flat(x):
                return x.rearrange("p a t -> p (a t)")

            def clear(norm):
                if norm:
                    pool.wait_ge(stats_done, norm)
                G.memset(sumsq[:], 0.0).then_inc(sumsq_done, 1)

            def add_square(norm, m):
                pool.wait_ge(sumsq_done, m + sumsq_base(norm) + 1)
                own.link(G.tensor_tensor(square[:], flat(h[:, at(m), :]), flat(h[:, at(m), :]), ALU.mult))
                G.tensor_tensor(sumsq[:], sumsq[:], square[:], ALU.add).then_inc(sumsq_done, 1)

            clear(0)
            for m in range(KT // 2):
                if m % 4 == 0:
                    pool.wait_ge(x_in[m // 4], 16)
                add_square(0, m)
            own.close(1)
            for index, ph in enumerate(phases):
                name = ph["name"]
                norm = next_norm(ph)
                if norm is not None:
                    clear(norm)
                if name == "A1":
                    def lru_split_x(head, hh):
                        for j in range(2):
                            pool.wait_ge(xc_hi, head * 2 + j + 1)
                            G.tensor_tensor(R[1][:, 1, 20 + j, :], xc[:, hh, j, :], R[1][:, 0, 20 + j, :].bitcast(F32),
                                            ALU.subtract).then_inc(xc_lo, 1)

                    def lru_early(head, hh):
                        pool.wait_ge(bank_free, head * 4 + 8)
                        own.link(G.tensor_tensor(ge, yv[:, hh], yv[:, hh], ALU.mult))
                        G.tensor_tensor(ge, ge, yv[:, hh], ALU.mult).then_inc(cube_done, 1)
                        pool.wait_ge(a_done, head * 2 + 2)
                        G.tensor_tensor(sq, av, av, ALU.mult).then_inc(asq_done, 1)

                    def lru_late(head, hh):
                        pool.wait_ge(y_hi, head + 1)
                        for j in range(2):
                            G.tensor_tensor(flat(R[1][:, 1, at(head * 2 + j), :]), yv[:, hh, j, :],
                                            flat(R[1][:, 0, at(head * 2 + j), :]).bitcast(F32), ALU.subtract
                                            ).then_inc(y_lo, 1)

                    def slot(head, hh, first=False):
                        if not first:
                            lru_early(head - 1, 1 - hh)
                        lru_split_x(head, hh)
                        if not first:
                            lru_late(head - 1, 1 - hh)

                    slot(0, 0, True)
                    slot(1, 1)
                    own.close()
                    with pool.Fori(1, LRU_HEADS // 2) as it:
                        own.begin(it - 1, 2)
                        slot(it * 2, 0)
                        slot(it * 2 + 1, 1)
                    own.close(LRU_HEADS // 2 - 1)
                    lru_early(LRU_HEADS - 1, 1)
                    lru_late(LRU_HEADS - 1, 1)
                    own.close()
                elif name == "F1":
                    f0 = ph["layer"] * FF_TILES + ph["half"] * HALF
                    dst = R[1 - source(ph)]
                    with pool.Fori(0, ph["iters"]) as it:
                        for j in range(2):
                            pool.wait_ge(mid_hi, it * 2 + f0 + j + 1)
                            G.tensor_tensor(flat(dst[:, 1, at(it * 2 + j), :]), swi_u[:, j, :],
                                            flat(dst[:, 0, at(it * 2 + j), :]).bitcast(F32), ALU.subtract
                                            ).then_inc(mid_ready, 1)
                elif name == "B1":
                    g0 = ph["half"] * 4

                    def ce(group):
                        pool.wait_ge(ebc_done, group + 1)
                        pool.wait_ge(silu_done, group * 6 + 2)
                        G.tensor_tensor(ebc, ebc, ca[:, 1:2, CHUNK:SEQ].broadcast_to([P, GROUP_HEADS, CHUNK]), ALU.mult
                                        ).then_inc(ce_done, 1)

                    def y_square(group):
                        for j in range(4):
                            pool.wait_ge(yz_done, group * 4 + j + 1)
                            G.tensor_tensor(ysq[:, j, :], zt[:, j, :], zt[:, j, :], ALU.mult).then_inc(ysq_done, 1)

                    def y_split(group, local):
                        for j in range(4):
                            pool.wait_ge(yn_hi, group * 4 + j + 1)
                            G.tensor_tensor(flat(R[0][:, 1, at(local * 4 + j), :]), zt[:, j, :],
                                            flat(R[0][:, 0, at(local * 4 + j), :]).bitcast(F32), ALU.subtract
                                            ).then_inc(yn_lo, 1)
                    ce(g0)
                    with pool.Fori(1, 4) as it:
                        y_square(it + (g0 - 1))
                        y_split(it + (g0 - 1), it - 1)
                        ce(it + g0)
                    y_square(g0 + 3)
                    y_split(g0 + 3, 3)
                if norm is not None:
                    if name == "PL":
                        base = ph["layer"] * KT
                        per = 1
                        done = h_done
                    else:
                        base, done = ph["group0"] + 4, bank_free
                    with pool.Fori(0, KT) as m:
                        own.begin(m, 1)
                        pool.wait_ge(done, m + base + 1)
                        add_square(norm, m)
                    own.close(KT)



def blocks_of(w):
    k, m = w.shape
    return w.reshape(k // P, P, m // P, P).transpose(2, 0, 1, 3)


def pieces_of(blocks, widths):
    import numpy as np
    out, b = [], 0
    for w in widths:
        out.append(blocks[:, b:b + w].transpose(0, 2, 1, 3).reshape(blocks.shape[0], -1))
        b += w
    assert b == blocks.shape[1]
    return np.concatenate(out, axis=1)


def columns(v):
    return v.reshape(-1, P).T


def lay_out(a):
    import numpy as np
    w = {n: widths for n, _, _, _, widths, _ in [(ph["name"], 0, 0, 0, ph["widths"], 0) for ph in phase_table()]}
    t = {}
    t["xT"] = a["x"][0].T.reshape(KT, P, SEQ).transpose(1, 0, 2)
    t["pT"] = a["p"][:, 0].transpose(0, 2, 1).reshape(2, 2, P, SEQ).transpose(0, 2, 1, 3).reshape(2, P, 2 * SEQ)
    t["gains"] = np.concatenate([columns(a[n][l]) for l in range(2) for n in ("norm_mix_g", "norm_ffn_g", "norm_ple_g")]
                                + [columns(a["final_norm_g"])], axis=1)
    taps = a["a_conv_w"][0].reshape(4, KT, P).transpose(2, 1, 0)
    t["apar"] = np.concatenate([taps] + [columns(v.reshape(-1))[:, :, None] for v in
                                         (a["a_conv_b"], a["a_b_gate_r"], a["a_b_gate_i"], a["a_lambda"])], axis=2)
    order = [[32 + g, 40 + g] + [4 * g + j for j in range(4)] for g in range(GROUPS)]
    conv = np.concatenate([a["b_conv_w"][0], a["b_conv_b"]], axis=0).reshape(5, 48, P).transpose(2, 1, 0)
    conv = conv[:, order].reshape(P, GROUPS, 30)
    dskip = columns(np.repeat(a["b_d_skip"][0], 64)).reshape(P, GROUPS, 4)
    t["bpar"] = np.concatenate([conv, dskip, columns(a["b_norm_g"][0]).reshape(P, GROUPS, 4)], axis=2)
    t["hpar"] = np.stack([a["b_dt_bias"][0], a["b_a_log"][0]], axis=1)
    win = blocks_of(a["a_w_in"][0])
    t["A10"] = pieces_of(np.stack([win[[4 * i, 4 * i + 1, 16 + 4 * i, 17 + 4 * i, 4 * i + 2, 4 * i + 3, 18 + 4 * i,
                                        19 + 4 * i]].reshape(-1, P, P) for i in range(4)]), w["A1"])
    gates = []
    for head in range(LRU_HEADS):
        bs = [blocks_of(a[n][0, head])[m, k] for n in ("a_w_gate_r", "a_w_gate_i") for m in range(2) for k in range(2)]
        gates.append(np.stack(bs, axis=1).reshape(P, 1024))
    t["gates"] = np.stack(gates)
    t["A20"] = pieces_of(blocks_of(a["a_w_out"][0]).reshape(4, 4 * KT, P, P), w["A2"])
    bw = a["b_w_in"][0]
    zt, xt = blocks_of(bw[:, :4096]), blocks_of(bw[:, 4096:10240])
    t["B11"] = pieces_of(np.stack([np.concatenate([xt[order[g]], zt[4 * g:4 * g + 4]]).reshape(-1, P, P)
                                   for g in range(GROUPS)]), w["B1"])
    dt = np.concatenate([bw[:, 10240:], bw[:, 10240:]], axis=1)
    t["dtw"] = dt.reshape(KT, P, P).transpose(1, 0, 2).reshape(P, KT * P)
    bo = blocks_of(a["b_w_out"][0])
    t["B21"] = pieces_of(bo.reshape(4, 4, 2, 16, P, P).transpose(2, 0, 1, 3, 4, 5).reshape(8, -1, P, P), w["B2"])
    for l in range(2):
        g, u = blocks_of(a["ffn_w_gate"][l]), blocks_of(a["ffn_w_up"][l])
        t[f"F1{l}"] = pieces_of(np.stack([g, u], axis=1).reshape(FF_TILES // 2, -1, P, P), w["F1"])
        d = blocks_of(a["ffn_w_down"][l])
        t[f"F2{l}"] = pieces_of(d.reshape(4, 4, 2, HALF, P, P).transpose(2, 0, 1, 3, 4, 5).reshape(8, -1, P, P), w["F2"])
        e = np.concatenate([blocks_of(a["ple_w_gate"][l]), blocks_of(a["ple_w_proj"][l])], axis=1)
        t[f"PL{l}"] = pieces_of(e.reshape(8, -1, P, P), w["PL"])
    return {k: np.ascontiguousarray(v) for k, v in t.items()}


STOP = None


def kernel(**inputs):
    import numpy as _np
    import concourse.bacc as _bacc
    from concourse.bass_utils import run_bass_kernel_spmd as _run

    laid = lay_out({k: _np.asarray(v) for k, v in inputs.items()})
    nc = _bacc.Bacc("TRN2", target_bir_lowering=False, num_devices=1)
    arrays = {f"in_{k}": v for k, v in laid.items()}
    t = {k: nc.dram_tensor(f"in_{k}", v.shape, F32, kind="ExternalInput").ap() for k, v in laid.items()}
    out = nc.dram_tensor("out_hT", (P, KT, SEQ), F32, kind="ExternalOutput").ap()
    trunk(nc, t, out, STOP)
    got = _run(nc, [arrays], core_ids=[0]).results[0]["out_hT"]
    return _np.ascontiguousarray(got.transpose(1, 0, 2).reshape(D, SEQ).T)[None]
```

```python
from contextlib import ExitStack

import concourse.bass as bass
from concourse import mybir

F32 = mybir.dt.float32
F32R = mybir.dt.float32r
ALU = mybir.AluOpType
ACT = mybir.ActivationFunctionType

P = 128
SEQ = 256
D = 2048
KT = D // P
EPS = 1e-6
ARENA = 11464
FF_TILES = 44
HALF = FF_TILES // 2
LRU_HEADS = 8
GROUPS = 8
HEADS = 64
GROUP_HEADS = HEADS // GROUPS
CHUNK = 128
RING = 4
LEAD = 3
BLOCK = P
PIECE = 8
LAST_HEAD = {0: (0, 1, 2), 1: (3, 4), 2: (5, 6), 3: (7,)}
WIDE = ("A1", "A2", "F1", "F2", "B2")
GELU_C = 0.7978845608028654
BANKS4 = [2, 3, 0, 1]
BANKS2 = [0, 1]

GAINS = 7 * KT
A_PAR = 8
B_PAR = 38


def phase_table():
    t = [("A1", 0, 0, 4, [8] * 16, 8), ("A2", 0, 0, 4, [8] * 8, 4)]
    for layer in range(2):
        if layer == 1:
            for half in range(2):
                t.append(("B1", 1, half, 4, [8] * 20, 10))
                t.append(("B2", 1, half, 4, [8] * 8, 4))
        for half in range(2):
            t.append(("F1", layer, half, HALF // 2, [8] * 8, 4))
            t.append(("F2", layer, half, 4, [6, 5, 6, 5] * 4, 4))
        t.append(("PL", layer, 0, 8, [5, 5, 4, 4] * 2, 4))
    out, piece, group = [], 0, 0
    for name, layer, half, iters, widths, groups in t:
        out.append(dict(name=name, layer=layer, half=half, iters=iters, widths=widths, groups=groups,
                        piece0=piece, group0=group))
        piece += iters * len(widths)
        group += iters * groups
    return out


class Chain:

    def __init__(self, engine, semaphore):
        self.engine, self.semaphore, self.total = engine, semaphore, 0
        self.begin(0, 0)

    def begin(self, it, per_iteration):
        self.it, self.per, self.n = it, per_iteration, 0

    def mark(self, instruction):
        instruction.then_inc(self.semaphore, 1)
        self.n += 1
        return self.total + self.it * self.per + self.n

    def need(self, value):
        self.engine.wait_ge(self.semaphore, value)

    def link(self, instruction):
        self.need(self.mark(instruction))

    def latest(self):
        return self.total + self.it * self.per + self.n

    def close(self, iterations=1):
        assert self.per in (0, self.n), (self.per, self.n)
        self.total += iterations * self.n
        self.begin(0, 0)


def trunk(nc, t, out):
    with ExitStack() as ctx:
        def sb(name, shape, dt=F32):
            return ctx.enter_context(nc.sbuf_tensor(name, shape, dt))

        def sem(name):
            return ctx.enter_context(nc.semaphore(name))

        h = sb("h", [P, KT, SEQ])
        R = [sb(f"R{i}", [P, 2, HALF, SEQ], F32R) for i in range(2)]
        wraw = sb("wraw", [P, RING, PIECE * BLOCK])
        whi = sb("whi", [P, RING, PIECE * BLOCK], F32R)
        wlo = sb("wlo", [P, RING, PIECE * BLOCK], F32R)
        rinv = sb("rinv", [P, SEQ])
        rinvh = sb("rinvh", [P, SEQ])
        sumsq = sb("sumsq", [P, SEQ])
        square = sb("square", [P, SEQ])
        grms = sb("grms", [P, SEQ])
        ident = sb("ident", [P, P])
        ones = sb("ones", [P, P])
        causal = sb("causal", [P, CHUNK])
        gains = sb("gains", [P, GAINS])
        apar = sb("apar", [P, KT, A_PAR])
        bpar = sb("bpar", [P, GROUPS, B_PAR])
        hpar = sb("hpar", [HEADS, 2])
        arena = sb("arena", [P, ARENA])
        used = [0]

        def scratch(n):
            a = arena[:, used[0]:used[0] + n]
            used[0] += n
            assert used[0] <= ARENA
            return a

        praw = scratch(512)
        swi4 = scratch(1024)
        swi_g = swi4[:, 0:512].rearrange("p (j t) -> p j t", j=2)
        swi_t = swi4[:, 512:1024].rearrange("p (j t) -> p j t", j=2)
        swi_u = scratch(512).rearrange("p (j t) -> p j t", j=2)
        keep = used[0]
        graw = scratch(2048)
        xpad = scratch(2 * 260).rearrange("p (j t) -> p j t", j=2)
        xc = scratch(1024).rearrange("p (h j t) -> p h j t", h=2, j=2)
        yv = scratch(1024).rearrange("p (h j t) -> p h j t", h=2, j=2)
        ge = scratch(512).rearrange("p (j t) -> p j t", j=2)
        tr = scratch(512).rearrange("p (j t) -> p j t", j=2)
        ti = scratch(512).rearrange("p (j t) -> p j t", j=2)
        av = scratch(512).rearrange("p (j t) -> p j t", j=2)
        sq = scratch(512).rearrange("p (j t) -> p j t", j=2)
        kt_a, kt_b, kt_c = scratch(16), scratch(16), scratch(16)
        sumsq2, square3 = ge[:, 0, :], ge[:, 1, :]
        square4 = swi4.rearrange("p (j t) -> p j t", j=4)
        used[0] = keep
        csb = scratch(2048).rearrange("p (e t) -> p e t", e=GROUP_HEADS)
        cpad = scratch(2 * 260).rearrange("p (j t) -> p j t", j=2)
        ebc = scratch(1024).rearrange("p (e t) -> p e t", e=GROUP_HEADS)
        xtok = scratch(1024).rearrange("p (c n) -> p c n", c=2)
        ysq = xtok.rearrange("p c (j t) -> p (c j) t", j=2)
        xdec = scratch(512)
        state = scratch(512)
        ca = scratch(6 * SEQ).rearrange("p (n t) -> p n t", n=6)
        zt = scratch(4 * SEQ).rearrange("p (n t) -> p n t", n=4)
        cth = scratch(2 * SEQ).rearrange("p (n t) -> p n t", n=2)
        btok = scratch(P)
        cbm = scratch(2 * CHUNK).rearrange("p (c l) -> p c l", c=2)
        cst = scratch(2 * HEADS).rearrange("p (c e) -> p c e", c=2)
        dtt = scratch(2 * HEADS).rearrange("p (c e) -> p c e", c=2)
        wdt = scratch(HEADS)
        dt_x, dt_e, dt_w, dt_z = [xtok[0:HEADS, c, n * SEQ:(n + 1) * SEQ] for c in range(2) for n in range(2)]
        dt_r, dt_v, dt_cs, dt_one = [zt[0:HEADS, n, :] for n in range(4)]
        dt_dec = xdec[0:HEADS, 0:CHUNK]

        bank = [ctx.enter_context(nc.psum_tensor(f"bank{i}", [P, 512], F32)) for i in range(8)]

        assert used[0] <= ARENA
        cs_dram = nc.dram_tensor("cs_rows", [HEADS, SEQ], F32, kind="Internal").ap()

        params_in = sem("params_in")
        gains_in = sem("gains_in")
        x_in = [sem(f"x_in{c}") for c in range(4)]
        p_in = sem("p_in")
        w_landed = [sem(f"w_landed{i}") for i in range(RING)]
        g_landed = sem("g_landed")
        w_hi, w_lo, w_used, bank_free = sem("w_hi"), sem("w_lo"), sem("w_used"), sem("bank_free")
        g_hi, g_lo, g_used = sem("g_hi"), sem("g_lo"), sem("g_used")
        const_done = sem("const_done")
        dve_own, act_own, pool_own = sem("dve_own"), sem("act_own"), sem("pool_own")
        u0_hi, square4_done = sem("u0_hi"), sem("square4_done")
        uh_done, u_ready = sem("uh_done"), sem("u_ready")
        sumsq2_done = sem("sumsq2_done")
        yz_done = sem("yz_done")
        sumsq_done, stats_done, var_done, rinv_done = sem("sumsq_done"), sem("stats_done"), sem("var_done"), sem("rinv_done")
        tanh_done, mid_done, mid_hi, mid_ready = sem("tanh_done"), sem("mid_done"), sem("mid_hi"), sem("mid_ready")
        p_hi, p_lo = sem("p_hi"), sem("p_lo")
        ple_t, h_done = sem("ple_t"), sem("h_done")
        softexp_in, softexp_out = sem("softexp_in"), sem("softexp_out")
        kk_done = sem("kk_done")
        xc_done, xc_hi, xc_lo = sem("xc_done"), sem("xc_hi"), sem("xc_lo")
        gate_t, a_done, e_done, asq_done, s_done, mult_done = (sem("gate_t"), sem("a_done"), sem("e_done"),
                                                               sem("asq_done"), sem("s_done"), sem("mult_done"))
        cube_done, gelu_q, gelu_t, y_done, y_hi, y_lo = sem("cube_done"), sem("gelu_q"), sem("gelu_t"), sem("y_done"), sem("y_hi"), sem("y_lo")
        last_square = sem("last_square")
        ysum_done = sem("ysum_done")
        gated_done, input_done = sem("gated_done"), sem("input_done")
        cs_done0 = sem("cs_done0")
        dt_mm, cs_done, cs_out, cs_in = sem("dt_mm"), sem("cs_done"), sem("cs_out"), sem("cs_in")
        a_exp, dec_exp, wdec_done, col_t, col_done = (sem("a_exp"), sem("dec_exp"),
                                                              sem("wdec_done"), sem("col_t"), sem("col_done"))
        conv_done, conv_t, silu_done = sem("conv_done"), sem("conv_t"), sem("silu_done")
        z_t, ebc_done, exp_done, ce_done, sc_done = sem("z_t"), sem("ebc_done"), sem("exp_done"), sem("ce_done"), sem("sc_done")
        turned, xtok_done, xdec_done, state_mm, state_done = (sem("turned"), sem("xtok_done"),
                                                                       sem("xdec_done"), sem("state_mm"), sem("state_done"))
        y_mm, y_read, ysq_done, gstat_mm, gvar_done, grinv_done = (sem("y_mm"), sem("y_read"), sem("ysq_done"),
                                                                   sem("gstat_mm"), sem("gvar_done"), sem("grinv_done"))
        yn_done, yn_hi, yn_lo = sem("yn_done"), sem("yn_hi"), sem("yn_lo")
        out_ready, out_done = sem("out_ready"), [sem("out_done0"), sem("out_done1")]

        phases = phase_table()

        def at(expr, n=1):
            return bass.ds(expr, n)

        def steps(engine, ph, body, chain, per):
            chain.close()
            body(0, True)
            chain.close()
            with engine.Fori(1, ph["iters"] - 1) as it:
                chain.begin(it - 1, per)
                body(it, False)
            chain.begin(ph["iters"] - 2, per)
            body(ph["iters"] - 1, False)
            chain.close(ph["iters"] - 1)

        def width_of(index, ph, q, last):
            w = ph["widths"]
            if q + LEAD < len(w):
                return w[q + LEAD]
            if not last:
                return w[q + LEAD - len(w)]
            return phases[index + 1]["widths"][q + LEAD - len(w)] if index + 1 < len(phases) else 0

        def norm_of(ph):
            return {("A1", 0): 0, ("F1", 0): 1, ("PL", 0): 2, ("B1", 1): 3, ("F1", 1): 4, ("PL", 1): 5}[
                (ph["name"], ph["layer"])] if ph["name"] in ("A1", "F1", "PL", "B1") and ph["half"] == 0 else None

        def next_norm(ph):
            return {("A2", 0, 0): 1, ("F2", 0, 1): 2, ("PL", 0, 0): 3, ("B2", 1, 1): 4, ("F2", 1, 1): 5,
                    ("PL", 1, 0): 6}.get((ph["name"], ph["layer"], ph["half"]))

        u_buf = {("A1", 0): 0, ("F1", 0): 0, ("PL", 0): 0, ("B1", 1): 1, ("F1", 1): 1, ("PL", 1): 1}

        def source(ph):
            name, layer = ph["name"], ph["layer"]
            if name == "A2":
                return 1
            if name == "B2":
                return 0
            if name == "F2":
                return 1 - u_buf[("F1", layer)]
            return u_buf[(name, layer)]

        def sumsq_base(norm):
            return norm * (KT + 1) - (4 if norm else 0)

        def next_u(norm):
            return {1: 0, 2: 0, 3: 1, 4: 1, 5: 1}[norm]

        block = ctx.enter_context(nc.Block())

        @block.sync
        def _(sp):
            def load_x(*parts):
                for c in parts:
                    sp.dma_start(h[:, 4 * c:4 * c + 4, :], t["xT"][:, 4 * c:4 * c + 4, :]).then_inc(x_in[c], 16)

            sp.dma_start(gains[:], t["gains"]).then_inc(gains_in, 16)
            for index, ph in enumerate(phases):
                src, widths, n = t[ph["name"] + str(ph["layer"])], ph["widths"], len(ph["widths"])
                src0 = ph["half"] * ph["iters"]

                def body(it, first, ph=ph, src=src, widths=widths, n=n, src0=src0, index=index):
                    at0 = 0
                    for q, w in enumerate(widths):
                        p = it * n + ph["piece0"] + q
                        if index or q >= RING or not first:
                            sp.wait_ge(w_lo, p - RING + 1)
                        sp.dma_start(wraw[:, q % RING, 0:w * BLOCK],
                                     src[at(it + src0), at0:at0 + P * w * BLOCK].rearrange("o (p c) -> (o p) c", p=P)
                                     ).then_inc(w_landed[q % RING], 16)
                        at0 += P * w * BLOCK
                        if index == 0 and first and q == 0:
                            load_x(0, 1, 2)
                        if index == 0 and first and q == 1:
                            load_x(3)
                        if index == 0 and first and q == 3:
                            for dst, part in ((apar, "apar"), (bpar, "bpar"), (hpar, "hpar")):
                                sp.dma_start(dst[:], t[part]).then_inc(params_in, 16)
                        if ph["name"] == "A1" and q % 8 == 2:
                            head = it * 2 + q // 8
                            if not (first and q == 2):
                                sp.wait_ge(g_lo, head)
                            sp.dma_start(graw[:, 0:1024], t["gates"][at(head)].rearrange("o p c -> (o p) c")
                                         ).then_inc(g_landed, 16)
                        if ph["name"] == "B1" and q == (13 if first and ph["half"] == 0 else 10):
                            group = it + ph["half"] * 4
                            if first and ph["half"] == 0:
                                sp.wait_ge(cs_out, 16)
                            else:
                                sp.wait_ge(y_mm, group * 2)
                            sp.dma_start(csb, cs_dram[at(group * GROUP_HEADS, GROUP_HEADS), :]
                                         .rearrange("e t -> (e t)").rearrange("(o n) -> o n", o=1)
                                         .broadcast_to([P, GROUP_HEADS * SEQ]).rearrange("p (e t) -> p e t", e=GROUP_HEADS)
                                         ).then_inc(cs_in, 16)
                if ph["name"] == "F2" and ph["half"] == 1:
                    if ph["layer"] == 1:
                        sp.wait_ge(p_lo, 1)
                    sp.dma_start(praw, t["pT"][ph["layer"]]).then_inc(p_in, 16)
                if ph["name"] == "F2" and ph["half"] == 1 and ph["layer"] == 0:
                    sp.wait_ge(g_lo, LRU_HEADS)
                    sp.dma_start(graw, t["dtw"]).then_inc(g_landed, 16)
                body(0, True)
                with sp.Fori(1, ph["iters"]) as it:
                    body(it, False)
            for m in range(KT):
                sp.wait_ge(out_ready, m + 1)
                sp.dma_start(out[:, m, :], h[:, m, :]).then_inc(out_done[m % 2], 16)
            for s in out_done:
                sp.wait_ge(s, 16 * KT // 2)

        @block.tensor
        def _(pe):
            def three(dst, hi_w, lo_w, hi_x, lo_x, first, last):
                nc.tensor.matmul(dst, hi_w, hi_x, start=first, stop=False)
                nc.tensor.matmul(dst, hi_w, lo_x, start=False, stop=False)
                return nc.tensor.matmul(dst, lo_w, hi_x, start=False, stop=last)

            def piece(ph, it, q, blocks):
                p = it * len(ph["widths"]) + ph["piece0"] + q
                pe.wait_ge(w_lo, p + 1)
                for b, (before, dst, src, k, first, last) in enumerate(blocks):
                    for s, v in before:
                        pe.wait_ge(s, v)
                    cols = slice(b * BLOCK, (b + 1) * BLOCK)
                    if ph["name"] not in WIDE:
                        mm = three(dst[:, 0:SEQ], whi[:, q % RING, cols], wlo[:, q % RING, cols], src[:, 0, k, :],
                                   src[:, 1, k, :], first, last)
                        continue
                    nc.tensor.matmul(dst.rearrange("p (s t) -> p s t", s=2), whi[:, q % RING, cols], src[:, :, k, :],
                                     start=first, stop=False)
                    mm = nc.tensor.matmul(dst[:, 0:SEQ], wlo[:, q % RING, cols], src[:, 0, k, :], start=False, stop=last)
                mm.then_inc(w_used, 1)

            def free(ph, it, j):
                n = it * ph["groups"] + ph["group0"] + j
                return (bank_free, n + (1 if ph["name"] != "B1" else 3))

            def matmul_groups(ph, it, operand_ready):
                src, name = R[source(ph)], ph["name"]
                kts = {"F2": HALF}.get(name, KT)
                banks = BANKS2 if name == "B1" else BANKS4
                items = []
                if name in ("A2", "B2"):
                    for k0 in (0, KT // 2):
                        for j in range(4):
                            for k in range(k0, k0 + KT // 2):
                                before = [free(ph, it, j)] if k == 0 else []
                                if j == 0:
                                    before += operand_ready(k)
                                items.append((before, bank[banks[j]][:], src, k, k == 0, k == KT - 1))
                    return items
                for j in range(ph["groups"]):
                    if name == "PL" and j % 2:
                        for k in range(2):
                            items.append(([free(ph, it, j)] + [(p_lo, ph["layer"] + 1)] if k == 0 else [],
                                          bank[banks[j % 4]][:], src, 20 + k, k == 0, k == 1))
                        continue
                    for k in range(kts):
                        before = [free(ph, it, j)] if k == 0 else []
                        if j == 0:
                            before += operand_ready(k)
                        items.append((before, bank[banks[j % len(banks)]][:], src, k, k == 0, k == kts - 1))
                return items

            pe.wait_ge(const_done, 3)
            mids = 0
            for index, ph in enumerate(phases):
                name, norm = ph["name"], norm_of(ph)
                if name in ("A1", "F1", "PL", "B1"):
                    number = {("A1", 0): 0, ("F1", 0): 1, ("PL", 0): 2, ("B1", 1): 3, ("F1", 1): 4, ("PL", 1): 5}[
                        (name, ph["layer"])]
                    base, tiles, ready = 16 * number, KT, u_ready
                elif name == "A2":
                    base, tiles, ready = 0, KT, y_lo
                elif name == "B2":
                    base, tiles, ready = 16 * ph["half"], KT, yn_lo
                else:
                    base, tiles, ready = mids, HALF, mid_ready
                    mids += HALF

                ahead = {"A1": 1, "A2": KT // 2, "B2": KT // 2}.get(name, tiles - 4)

                def operand_ready(k, base=base, ready=ready, ahead=ahead):
                    if k == 0:
                        return [(ready, base + ahead)]
                    return [(ready, base + k + 1)] if k >= ahead else []

                def decay_products(base=base):
                    pe.wait_ge(g_lo, LRU_HEADS + 1)
                    for k in range(KT):
                        wr = R[1] if k < 8 else R[0]
                        c = slice((k % 8) * 128 % 256, (k % 8) * 128 % 256 + 128)
                        tile = 16 + (k % 8) // 2
                        mm = three(bank[7][:, 0:SEQ], wr[:, 0, tile, c], wr[:, 1, tile, c], R[1][:, 0, k, :],
                                   R[1][:, 1, k, :], k == 0, k == KT - 1)
                    mm.then_inc(dt_mm, 1)

                def decay_columns():
                    pe.wait_ge(wdec_done, 1)
                    for c in range(2):
                        nc.tensor.transpose(bank[5][:, c * 64:c * 64 + 64], dt_cs[:, c * CHUNK:(c + 1) * CHUNK],
                                            ident[0:HEADS, 0:HEADS])
                        nc.tensor.transpose(bank[5][:, 128 + c * 64:192 + c * 64], dt_v[:, c * CHUNK:(c + 1) * CHUNK],
                                            ident[0:HEADS, 0:HEADS])
                    nc.tensor.transpose(bank[5][:, 256:320], dt_dec, ident[0:HEADS, 0:HEADS]).then_inc(col_t, 1)

                def body(it, first, ph=ph, name=name, norm=norm, operand_ready=operand_ready):
                    items = matmul_groups(ph, it, operand_ready)
                    done = 0
                    for q, w in enumerate(ph["widths"]):
                        piece(ph, it, q, items[done:done + w])
                        done += w
                        if norm is not None and first and q == (3 if norm == 0 else 1):
                            pe.wait_ge(sumsq_done, sumsq_base(norm + 1))
                            if norm == 0:
                                pe.wait_ge(sumsq2_done, 1)
                                nc.tensor.matmul(bank[6][:, 0:SEQ], ones[:], sumsq2, start=True, stop=False)
                            nc.tensor.matmul(bank[6][:, 0:SEQ], ones[:], sumsq[:], start=norm != 0, stop=True
                                             ).then_inc(stats_done, 1)
                        if name == "B2" and first and q == 2:
                            group_stats(ph["half"] * 4 + 3)
                        if name == "B1" and ph["half"] == 0 and first:
                            if q == 1:
                                decay_products()
                            if q == 9:
                                decay_columns()
                        if name == "A1" and q % 8 == 7:
                            head = it * 2 + q // 8
                            pe.wait_ge(g_lo, head + 1)
                            pe.wait_ge(xc_lo, head * 2 + 2)
                            if not (first and q == 7):
                                pe.wait_ge(gate_t, head * 4)
                            b = 0
                            for g in range(2):
                                for m in range(2):
                                    for k in range(2):
                                        tile, c = 16 + b // 2, slice((b % 2) * 128, (b % 2) * 128 + 128)
                                        mm = three(bank[4 + g][:, m * SEQ:(m + 1) * SEQ], R[1][:, 0, tile, c],
                                                   R[1][:, 1, tile, c], R[1][:, 0, 20 + k, :], R[1][:, 1, 20 + k, :],
                                                   k == 0, k == 1)
                                        b += 1
                            mm.then_inc(g_used, 1)
                        if name == "B1":
                            group = it + ph["half"] * 4
                            if q == 4 and not first:
                                group_stats(group - 1)
                            if q == 14:
                                pe.wait_ge(silu_done, group * 6 + 6)
                                if not (first and ph["half"] == 0):
                                    pe.wait_ge(y_read, group * 4)
                                for c in range(2):
                                    nc.tensor.matmul(bank[4][:, c * CHUNK:(c + 1) * CHUNK],
                                                     ca[:, 0, c * CHUNK:(c + 1) * CHUNK],
                                                     ca[:, 1, c * CHUNK:(c + 1) * CHUNK], start=True, stop=True)
                                nc.tensor.transpose(bank[4][:, 256:384], ca[:, 0, 0:CHUNK], ident[:])
                                for c in range(2):
                                    for j in range(4):
                                        mm = nc.tensor.transpose(bank[5 + c][:, j * P:(j + 1) * P],
                                                                 ca[:, 2 + j, c * CHUNK:(c + 1) * CHUNK], ident[:])
                                mm.then_inc(turned, 1)
                            if q == 16:
                                pe.wait_ge(xdec_done, group + 1)
                                nc.tensor.matmul(bank[5][:, 0:512], btok, xdec, start=True, stop=True
                                                 ).then_inc(state_mm, 1)
                            if q in (17, 19):
                                pair0 = 0 if q == 17 else 2
                                pe.wait_ge(sc_done, group * 2 + q // 2 - 7)
                                if q == 17:
                                    pe.wait_ge(ce_done, group + 1)
                                    pe.wait_ge(state_done, group + 1)
                                for j in range(pair0, pair0 + 2):
                                    dst = bank[6 if j < 2 else 4]
                                    for e in range(2):
                                        head, rows = 2 * j + e, slice(64 * e, 64 * e + 64)
                                        cols = (j % 2) * SEQ
                                        ch = slice(head * 64, head * 64 + 64)
                                        nc.tensor.matmul(dst[rows, cols:cols + CHUNK], xtok[:, 0, ch],
                                                         csb[:, head, 0:CHUNK], start=True, stop=True)
                                        nc.tensor.matmul(dst[rows, cols + CHUNK:cols + SEQ], xtok[:, 1, ch],
                                                         csb[:, head, CHUNK:SEQ], start=True, stop=False)
                                        mm = nc.tensor.matmul(dst[rows, cols + CHUNK:cols + SEQ], state[:, ch],
                                                              ebc[:, head, :], start=False, stop=True)
                                mm.then_inc(y_mm, 1)

                def group_stats(group):
                    pe.wait_ge(ysum_done, group + 1)
                    nc.tensor.matmul(bank[7][:, 0:SEQ], ones[:], ysq[:, 0, :], start=True, stop=True).then_inc(gstat_mm, 1)

                body(0, True)
                with pe.Fori(1, ph["iters"]) as it:
                    body(it, False)
            pe.wait_ge(sumsq_done, sumsq_base(7) - 1)
            nc.tensor.matmul(bank[6][:, 0:SEQ], ones[:], sumsq[:], start=True, stop=False)
            pe.wait_ge(last_square, 1)
            nc.tensor.matmul(bank[6][:, 0:SEQ], ones[:], swi_u[:, 0, :], start=False, stop=True).then_inc(stats_done, 1)

        @block.scalar
        def _(act):
            own = Chain(act, act_own)

            def hi(ph_piece, q, w, early=False):
                slot = q % RING
                act.wait_ge(w_landed[slot], (ph_piece - slot) * (16 // RING) + 16)
                if not early:
                    act.wait_ge(w_used, ph_piece - RING + 1)
                nc.scalar.activation(whi[:, slot, 0:w * BLOCK], wraw[:, slot, 0:w * BLOCK], ACT.Copy).then_inc(w_hi, 1)

            def softexp(n, dst, src):
                act.wait_ge(softexp_in, n)
                nc.scalar.activation(dst, src, ACT.Exp).then_inc(softexp_out, 1)

            def norm(k):
                act.wait_ge(var_done, k + 1)
                nc.scalar.activation(rinv[:], rinvh[:], ACT.Sqrt).then_inc(rinv_done, 1)

            act.wait_ge(gains_in, 16)
            for c in range(4):
                if c < 3:
                    hi(c, c, 8, early=True)
                act.wait_ge(x_in[c], 16)
                for m in range(4 * c, 4 * c + 4):
                    nc.scalar.activation(R[0][:, 0, m, :], h[:, m, :], ACT.Copy, scale=gains[:, m:m + 1]
                                         ).then_inc(u0_hi, 1)
            nc.scalar.activation(square4, h[:, 8:12, :], ACT.Square).then_inc(square4_done, 1)
            for index, ph in enumerate(phases):
                name, n = ph["name"], len(ph["widths"])
                if name == "PL":
                    src = R[u_buf[("PL", ph["layer"])]]
                    act.wait_ge(p_in, 16 * (ph["layer"] + 1))
                    nc.scalar.activation(src[:, 0, 20:22, :], praw.rearrange("p (k t) -> p k t", k=2), ACT.Copy
                                         ).then_inc(p_hi, 1)

                def decay_steps(q):
                    if q == 2:
                        softexp(2, dt_e, dt_w)
                        nc.scalar.activation(hpar[:, 1:2], hpar[:, 1:2], ACT.Exp).then_inc(a_exp, 1)
                    elif q == 6:
                        act.wait_ge(cs_done, 1)
                        act.dma_start(cs_dram, dt_cs).then_inc(cs_out, 16)
                        nc.scalar.activation(dt_dec, dt_cs[:, 0:CHUNK], ACT.Exp, bias=dt_cs[:, CHUNK - 1:CHUNK],
                                             scale=-1.0).then_inc(dec_exp, 1)

                def split_dt_weights():
                    act.wait_ge(g_landed, 16 * (LRU_HEADS + 1))
                    for r, lo in ((1, 0), (0, 1024)):
                        last = nc.scalar.activation(R[r][:, 0, 16:20, :],
                                                    graw[:, lo:lo + 1024].rearrange("p (k t) -> p k t", k=4), ACT.Copy)
                    last.then_inc(g_hi, 1)

                def gates(head):
                    act.wait_ge(g_used, head + 1)
                    for g, dst in ((0, tr), (1, ti)):
                        for j in range(2):
                            nc.scalar.activation(dst[:, j, :], bank[4 + g][:, j * SEQ:(j + 1) * SEQ], ACT.Tanh,
                                                 bias=apar[:, at(head * 2 + j), 5 + g:6 + g].rearrange("p a b -> p (a b)"),
                                                 scale=0.5).then_inc(gate_t, 1)

                def decays(head):
                    act.wait_ge(gate_t, head * 4 + 2)
                    kk = [apar[:, at(head * 2 + j), 7:8].rearrange("p a b -> p (a b)") for j in range(2)]
                    for j in range(2):
                        nc.scalar.activation(av[:, j, :], tr[:, j, :], ACT.Exp, bias=kk[j], scale=kk[j]).then_inc(a_done, 1)
                    for j in range(2):
                        nc.scalar.activation(tr[:, j, :], tr[:, j, :], ACT.Tanh, bias=kk[j], scale=kk[j]).then_inc(e_done, 1)

                def mult(head):
                    act.wait_ge(s_done, head + 1)
                    nc.scalar.activation(sq, sq, ACT.Sqrt, scale=-1.0).then_inc(mult_done, 1)

                def gelu(head, hh):
                    act.wait_ge(gelu_q, head + 1)
                    nc.scalar.activation(ge, ge, ACT.Tanh, scale=GELU_C).then_inc(gelu_t, 1)

                def lru_y(head, hh):
                    act.wait_ge(y_done, head + 1)
                    nc.scalar.activation(R[1][:, 0, at(head * 2, 2), :], yv[:, hh], ACT.Copy).then_inc(y_hi, 1)

                def chain_step(head, hh, s):
                    if s == 0:
                        gates(head)
                    elif s == 1:
                        decays(head)
                    elif s == 3:
                        gelu(head, hh)
                    elif s == 5:
                        mult(head)
                    elif s == 7:
                        lru_y(head, hh)

                def body(it, first, ph=ph, name=name, n=n, index=index):
                    last = isinstance(it, int) and it == ph["iters"] - 1
                    for q in range(n):
                        p = it * n + ph["piece0"] + q
                        w = width_of(index, ph, q, last)
                        if w:
                            hi(p + LEAD, q + LEAD, w, early=first and index == 0 and q == 0)
                        if norm_of(ph) is not None and first and q == (2 if index == 0 else 1):
                            norm(norm_of(ph))
                        if name == "PL" and ph["layer"] == 0 and first and q == 5:
                            split_dt_weights()
                        if name == "A1" and first and q == 3:
                            softexp(1, kt_b, kt_a)
                        if name == "A1" and first and q == 7:
                            act.wait_ge(kk_done, 2)
                        if name == "A2" and first:
                            for s in LAST_HEAD.get(q, ()):
                                chain_step(LRU_HEADS - 1, 1, s)
                        if name == "B2" and first:
                            local = ph["half"] * 4 + 3
                            if q == 0:
                                z_tanh(4, 19, local, phases[index - 1]["group0"])
                            if q == 2:
                                group_rinv(local)
                            if q == 3:
                                group_hi(local, 3)
                        if name == "A1":
                            head, hh, s = it * 2 + q // 8, q // 8, q % 8
                            if not (first and q < 8):
                                chain_step(head - 1, 1 - hh, s)
                            if s in ((4, 5) if first and q < 8 else (3, 5)):
                                j = s // 5
                                act.wait_ge(xc_done, head * 2 + j + 1)
                                if not (first and q < 8):
                                    act.wait_ge(g_used, head)
                                nc.scalar.activation(R[1][:, 0, 20 + j, :], xc[:, hh, j, :], ACT.Copy).then_inc(xc_hi, 1)
                            if s == 4:
                                act.wait_ge(g_landed, head * 16 + 16)
                                if not (first and q < 8):
                                    act.wait_ge(g_used, head)
                                nc.scalar.activation(R[1][:, 0, 16:20, :],
                                                     graw[:, 0:1024].rearrange("p (k t) -> p k t", k=4), ACT.Copy
                                                     ).then_inc(g_hi, 1)
                        if name == "F1":
                            f = it * 2 + ph["layer"] * FF_TILES + ph["half"] * HALF
                            g = it * 4 + ph["group0"] + 4
                            if q in (2, 6):
                                j = q // 4
                                act.wait_ge(bank_free, g + 2 * j + 1)
                                nc.scalar.activation(swi_t[:, j, :], swi_g[:, j, :], ACT.Tanh).then_inc(tanh_done, 1)
                            if q in (4, 7):
                                j = q // 7
                                act.wait_ge(mid_done, f + j + 1)
                                nc.scalar.activation(R[1 - source(ph)][:, 0, at(it * 2 + j), :].rearrange("p a t -> p (a t)"),
                                                     swi_u[:, j, :], ACT.Copy).then_inc(mid_hi, 1)
                        if name == "PL" and q in (3, 7):
                            j = q // 4
                            g = it * 4 + ph["group0"] + 4
                            act.wait_ge(bank_free, g + 2 * j + 1)
                            nc.scalar.activation(swi_t[:, j, :], swi_g[:, j, :], ACT.Tanh).then_inc(ple_t, 1)
                        if name == "B1":
                            group = it + ph["half"] * 4
                            very_first = first and ph["half"] == 0
                            if very_first:
                                decay_steps(q)
                            if q == 0 and not first:
                                z_tanh(it, 19, group - 1)
                            if q == 6 and not first:
                                group_rinv(group - 1)
                            if q == 8 and not first:
                                group_hi(group - 1, it - 1)
                            if q % 2 == 0 and 2 <= q <= 12:
                                nt = q // 2 - 1
                                act.wait_ge(conv_done, group * 6 + nt + 1)
                                nc.scalar.activation(cth[:, nt % 2, :], ca[:, nt, :], ACT.Tanh).then_inc(conv_t, 1)
                            if q in (14, 16, 18):
                                z_tanh(it, q - 1, group)
                            if q == (11 if very_first else 9):
                                act.wait_ge(cs_in, group * 16 + 16)
                                if not very_first:
                                    act.wait_ge(y_mm, group * 2)
                                nc.scalar.activation(ebc, csb[:, :, CHUNK:SEQ], ACT.Exp).then_inc(ebc_done, 1)
                            if q in (11, 13, 15, 17):
                                if q == 11:
                                    if very_first:
                                        act.wait_ge(col_done, 1)
                                    act.wait_ge(ebc_done, group + 1)
                                e0 = q - 11
                                for e in (e0, e0 + 1):
                                    for c in range(2):
                                        r = nc.scalar.activation(csb[:, e, c * CHUNK:(c + 1) * CHUNK],
                                                                 csb[:, e, c * CHUNK:(c + 1) * CHUNK], ACT.Relu,
                                                                 bias=cst[:, c, at(group * GROUP_HEADS + e)], scale=-1.0)
                                own.link(r)
                                nc.scalar.activation(csb[:, e0:e0 + 2, :], csb[:, e0:e0 + 2, :], ACT.Exp, scale=-1.0
                                                     ).then_inc(exp_done, 1)
                            if q == 14:
                                act.wait_ge(turned, group + 1)
                                for c in range(2):
                                    nc.scalar.activation(xtok[:, c, :], bank[5 + c][:], ACT.Copy).then_inc(xtok_done, 1)
                            if q == 16:
                                act.wait_ge(state_mm, group + 1)
                                nc.scalar.activation(state, bank[5][:], ACT.Copy).then_inc(state_done, 1)

                def z_tanh(it, q, group, group0=ph["group0"]):
                    j = q // 2 - 6
                    act.wait_ge(bank_free, (it - (j == 3)) * 10 + group0 + 4 + q // 2 + 1)
                    nc.scalar.activation(cth[:, j % 2, :], zt[:, j, :], ACT.Tanh).then_inc(z_t, 1)

                def group_rinv(group):
                    act.wait_ge(gvar_done, group + 1)
                    nc.scalar.activation(grms[:], grms[:], ACT.Sqrt).then_inc(grinv_done, 1)

                def group_hi(group, local):
                    local = local * 4
                    for j in range(4):
                        act.wait_ge(yn_done, group * 4 + j + 1)
                        nc.scalar.activation(R[0][:, 0, at(local + j), :].rearrange("p a t -> p (a t)"), zt[:, j, :], ACT.Copy
                                             ).then_inc(yn_hi, 1)

                steps(act, ph, body, own, 4 if name == "B1" else 0)
            norm(6)

        @block.vector
        def _(dve):
            own = Chain(dve, dve_own)
            V = nc.vector

            def lo(p, q, w):
                slot = q % RING
                dve.wait_ge(w_hi, p + 1)
                V.tensor_tensor(wlo[:, slot, 0:w * BLOCK], wraw[:, slot, 0:w * BLOCK],
                                whi[:, slot, 0:w * BLOCK].bitcast(F32), ALU.subtract).then_inc(w_lo, 1)

            def softplus_head(x, e_in):
                own.link(V.tensor_scalar(e_in, x, -1.0, None, ALU.mult))
                V.tensor_tensor(e_in, e_in, x, ALU.min).then_inc(softexp_in, 1)

            def softplus_mid(n, e, w, z, r):
                dve.wait_ge(softexp_out, n)
                own.link(V.tensor_scalar(z, e, 2.0, None, ALU.add))
                own.link(V.reciprocal(r, z))
                own.link(V.tensor_tensor(w, e, r, ALU.mult))
                own.link(V.tensor_tensor(z, w, w, ALU.mult))

            def softplus_tail(x, w, z, r):
                own.link(V.tensor_scalar(r, z, 1.0 / 17, None, ALU.mult))
                for c in (15, 13, 11, 9, 7, 5, 3):
                    own.link(V.scalar_tensor_tensor(out=r, in0=r, scalar=1.0 / c, in1=z, op0=ALU.add, op1=ALU.mult))
                own.link(V.scalar_tensor_tensor(out=r, in0=r, scalar=1.0, in1=w, op0=ALU.add, op1=ALU.mult))
                own.link(V.tensor_scalar(x, x, 0.0, None, ALU.max))
                own.link(V.scalar_tensor_tensor(out=x, in0=r, scalar=2.0, in1=x, op0=ALU.mult, op1=ALU.add))

            def u_split(norm, m, count, buf):
                g = gains[:, at(m + norm * KT)]
                dst = R[buf]
                def tile(x):
                    return x.rearrange("p a t -> p (a t)")
                V.tensor_scalar(tile(dst[:, 0, at(m), :]), tile(h[:, at(m), :]), g, None, ALU.mult).then_inc(uh_done, 1)
                dve.wait_ge(uh_done, count)
                V.scalar_tensor_tensor(out=tile(dst[:, 1, at(m), :]), in0=tile(h[:, at(m), :]), scalar=g,
                                       in1=tile(dst[:, 0, at(m), :]).bitcast(F32), op0=ALU.mult, op1=ALU.subtract
                                       ).then_inc(u_ready, 1)

            def norm(k):
                dve.wait_ge(stats_done, k + 1)
                own.link(V.tensor_scalar(rinvh[:], bank[6][:, 0:SEQ], 1.0 / D, EPS, ALU.mult, ALU.add))
                V.reciprocal(rinvh[:], rinvh[:]).then_inc(var_done, 1)
                dve.wait_ge(rinv_done, k + 1)
                own.link(V.tensor_scalar(rinvh[:], rinv[:], 0.5, None, ALU.mult))

            for _ in range(4):
                dve.sem_inc(bank_free, 1)
            own.mark(V.memset(xpad, 0.0))
            dve.wait_ge(gains_in, 16)
            for c in range(4):
                if c < 3:
                    lo(c, c, 8)
                dve.wait_ge(x_in[c], 16)
                for m in range(4 * c, 4 * c + 4):
                    dve.wait_ge(u0_hi, m + 1)
                    V.scalar_tensor_tensor(out=R[0][:, 1, m, :], in0=h[:, m, :], scalar=gains[:, m:m + 1],
                                           in1=R[0][:, 0, m, :].bitcast(F32), op0=ALU.mult, op1=ALU.subtract
                                           ).then_inc(u_ready, 1)
            own.need(own.latest())
            own.close(1)
            def squares(m0):
                for m in range(m0, m0 + 2):
                    if m == KT - 4:
                        own.link(V.tensor_tensor(sumsq2, h[:, m, :], h[:, m, :], ALU.mult))
                        continue
                    own.link(V.tensor_tensor(square3, h[:, m, :], h[:, m, :], ALU.mult))
                    last = V.tensor_tensor(sumsq2, sumsq2, square3, ALU.add)
                    if m < KT - 1:
                        own.link(last)
                    else:
                        last.then_inc(sumsq2_done, 1)

            kk_w, kk_z, kk_r = (sq[:, 0, 0:16], sq[:, 0, 16:32], sq[:, 0, 32:48])

            def kk_steps(q):
                lam = apar[:, :, 7]
                if q == 2:
                    dve.wait_ge(params_in, 48)
                    own.link(V.tensor_scalar(kt_c, lam, -1.0, None, ALU.mult))
                    softplus_head(kt_c, kt_a)
                elif q == 6:
                    softplus_mid(1, kt_b, kk_w, kk_z, kk_r)
                    softplus_tail(kt_c, kk_w, kk_z, kk_r)
                    V.tensor_scalar(lam, kt_c, -4.0, None, ALU.mult).then_inc(kk_done, 1)
                    V.tensor_scalar(apar[:, :, 5:7], apar[:, :, 5:7], 0.5, None, ALU.mult).then_inc(kk_done, 1)
                    own.link(V.tensor_scalar(bpar[:, :, 0:30], bpar[:, :, 0:30], 0.5, None, ALU.mult))

            for index, ph in enumerate(phases):
                name, n = ph["name"], len(ph["widths"])
                if name == "PL":
                    src = R[u_buf[("PL", ph["layer"])]]
                    dve.wait_ge(p_hi, ph["layer"] + 1)
                    V.tensor_tensor(src[:, 1, 20:22, :], praw.rearrange("p (k t) -> p k t", k=2),
                                    src[:, 0, 20:22, :].bitcast(F32), ALU.subtract).then_inc(p_lo, 1)
                if name == "B1" and ph["half"] == 0:
                    own.mark(V.memset(cpad, 0.0))
                    own.link(V.memset(dt_one, 1.0))
                    dve.wait_ge(const_done, 3)
                own.close(1)

                def split_dt_weights():
                    dve.wait_ge(g_hi, LRU_HEADS + 1)
                    for r, at0 in ((1, 0), (0, 1024)):
                        last = V.tensor_tensor(R[r][:, 1, 16:20, :],
                                               graw[:, at0:at0 + 1024].rearrange("p (k t) -> p k t", k=4),
                                               R[r][:, 0, 16:20, :].bitcast(F32), ALU.subtract)
                    last.then_inc(g_lo, 1)

                def decay_steps(q):
                    if q == 2:
                        dve.wait_ge(dt_mm, 1)
                        own.link(V.tensor_tensor(dt_x, bank[7][0:HEADS, 0:SEQ], rinv[0:HEADS, :], ALU.mult))
                        own.link(V.tensor_scalar(dt_v, dt_x, hpar[:, 0:1], None, ALU.add))
                        softplus_head(dt_v, dt_w)
                    elif q == 3:
                        softplus_mid(2, dt_e, dt_w, dt_z, dt_r)
                    elif q == 4:
                        softplus_tail(dt_v, dt_w, dt_z, dt_r)
                        dve.wait_ge(a_exp, 1)
                        own.link(V.tensor_scalar(dt_x, dt_v, hpar[:, 1:2], -1.0, ALU.mult, ALU.mult))
                        V.tensor_tensor_scan(dt_cs[:, 0:CHUNK], dt_one[:, 0:CHUNK], dt_x[:, 0:CHUNK], 0.0, ALU.mult, ALU.add
                                             ).then_inc(cs_done0, 1)
                        dve.wait_ge(cs_done0, 1)
                        V.tensor_tensor_scan(dt_cs[:, CHUNK:SEQ], dt_one[:, CHUNK:SEQ], dt_x[:, CHUNK:SEQ], 0.0,
                                             ALU.mult, ALU.add).then_inc(cs_done, 1)
                    elif q == 7:
                        dve.wait_ge(dec_exp, 1)
                        V.tensor_tensor(dt_dec, dt_dec, dt_v[:, 0:CHUNK], ALU.mult).then_inc(wdec_done, 1)
                    elif q == 10:
                        dve.wait_ge(col_t, 1)
                        V.tensor_copy(cst, bank[5][:, 0:128].rearrange("p (c e) -> p c e", c=2)).then_inc(col_done, 1)
                        own.mark(V.tensor_copy(dtt, bank[5][:, 128:256].rearrange("p (c e) -> p c e", c=2)))
                        own.link(V.tensor_copy(wdt, bank[5][:, 256:320]))

                def flat(x):
                    return x.rearrange("p a t -> p (a t)")

                def fold(number, dst):
                    own.link(V.tensor_reduce(dst, bank[number][:].rearrange("p (s t) -> p t s", s=2), mybir.AxisListType.X, ALU.add))

                def conv(pad, dst, taps, bias, count, done):
                    own.link(V.tensor_scalar(dst, pad[:, 3:3 + SEQ], taps(3), bias, ALU.mult, ALU.add))
                    for k in (2, 1):
                        own.link(V.scalar_tensor_tensor(out=dst, in0=pad[:, k:k + SEQ], scalar=taps(k), in1=dst,
                                                        op0=ALU.mult, op1=ALU.add))
                    V.scalar_tensor_tensor(out=dst, in0=pad[:, 0:SEQ], scalar=taps(0), in1=dst, op0=ALU.mult,
                                           op1=ALU.add).then_inc(done, 1)

                def chain_step(head, hh, s):
                    if s == 2:
                        dve.wait_ge(cube_done, head + 1)
                        V.scalar_tensor_tensor(out=ge, in0=ge, scalar=0.044715, in1=yv[:, hh], op0=ALU.mult, op1=ALU.add
                                               ).then_inc(gelu_q, 1)
                    elif s == 4:
                        dve.wait_ge(asq_done, head + 1)
                        dve.wait_ge(e_done, head * 2 + 2)
                        V.scalar_tensor_tensor(out=sq, in0=sq, scalar=1.0, in1=tr, op0=ALU.add, op1=ALU.mult
                                               ).then_inc(s_done, 1)
                        dve.wait_ge(gate_t, head * 4 + 4)
                        V.scalar_tensor_tensor(out=ti, in0=ti, scalar=1.0, in1=xc[:, hh], op0=ALU.add, op1=ALU.mult
                                               ).then_inc(gated_done, 1)
                    elif s == 5:
                        dve.wait_ge(gelu_t, head + 1)
                        own.mark(V.scalar_tensor_tensor(out=ge, in0=ge, scalar=1.0, in1=yv[:, hh], op0=ALU.add, op1=ALU.mult))
                    elif s == 6:
                        dve.wait_ge(input_done, head + 1)
                        for j in range(2):
                            own.mark(V.tensor_tensor_scan(tr[:, j, :], av[:, j, :], ti[:, j, :], 0.0, ALU.mult, ALU.add))
                        own.need(own.latest())
                        V.scalar_tensor_tensor(out=yv[:, hh], in0=tr, scalar=0.25, in1=ge, op0=ALU.mult, op1=ALU.mult
                                               ).then_inc(y_done, 1)

                def body(it, first, ph=ph, name=name, n=n, index=index):
                    last = isinstance(it, int) and it == ph["iters"] - 1
                    for q in range(n):
                        p = it * n + ph["piece0"] + q
                        w = width_of(index, ph, q, last)
                        if w:
                            lo(p + LEAD, q + LEAD, w)
                        g0 = it * ph["groups"] + ph["group0"] + 4
                        if norm_of(ph) is not None and first and q == (2 if index == 0 else 1):
                            norm(norm_of(ph))
                        if name == "PL" and ph["layer"] == 0 and first and q == 6:
                            split_dt_weights()
                        if name == "A1" and first:
                            if q < 2:
                                squares(KT - 4 + 2 * q)
                            kk_steps(q)
                        if name == "A2" and first:
                            for s in LAST_HEAD.get(q, ()):
                                chain_step(LRU_HEADS - 1, 1, s)
                        if name == "B2" and first:
                            if q == 0:
                                z_silu(ph["half"] * 4 + 3, 3)
                                group_y(ph["half"] * 4 + 3)
                            if q == 2:
                                group_var(ph["half"] * 4 + 3)
                            if q == 3:
                                group_norm(ph["half"] * 4 + 3)
                        if name == "A1":
                            head, hh, s = it * 2 + q // 8, q // 8, q % 8
                            if not (first and q < 8):
                                chain_step(head - 1, 1 - hh, s)
                            group = ({3: 0, 4: 1, 5: 2, 7: 3} if first and q < 8 else {1: 0, 3: 1, 5: 2, 7: 3}).get(s)
                            if group is not None:
                                dve.wait_ge(w_used, p - s + 2 * group + 2)
                                src = BANKS4[group]
                            if group in (0, 1):
                                j = group
                                tile = head * 2 + j
                                row = xpad[:, j, 3:3 + SEQ]
                                fold(src, row)
                                V.tensor_tensor(row, row, rinv[:], ALU.mult).then_inc(bank_free, 1)
                                dve.wait_ge(bank_free, g0 + hh * 4 + j + 1)
                                conv(xpad[:, j], xc[:, hh, j, :],
                                     lambda k, tile=tile: flat(apar[:, at(tile), k:k + 1]), flat(apar[:, at(tile), 4:5]),
                                     tile, xc_done)
                            if group in (2, 3):
                                if group == 2 and not first:
                                    dve.wait_ge(y_lo, head * 2 - 2)
                                row = yv[:, hh, s // 2 - 2, :]
                                fold(src, row)
                                V.tensor_tensor(row, row, rinv[:], ALU.mult).then_inc(bank_free, 1)
                        if name in ("A2", "F2", "B2"):
                            per = n // 4
                            if q % per == per - 1 if name == "F2" else q >= 4:
                                j = q // per if name == "F2" else q - 4
                                m = it * 4 + j
                                dve.wait_ge(w_used, p + 1)
                                row = flat(h[:, at(m), :])
                                own.link(V.tensor_tensor(row, bank[BANKS4[j]][:, 0:SEQ], row, ALU.add))
                                V.tensor_tensor(row, bank[BANKS4[j]][:, SEQ:2 * SEQ], row, ALU.add).then_inc(bank_free, 1)
                                if next_norm(ph) is not None:
                                    dve.wait_ge(bank_free, g0 + j + 1)
                                    u_split(next_norm(ph), m, m + (next_norm(ph) - 1) * KT + 1, next_u(next_norm(ph)))
                        if name == "F1":
                            f = it * 2 + ph["layer"] * FF_TILES + ph["half"] * HALF
                            j = q // 4
                            if q in (1, 5):
                                dve.wait_ge(w_used, p + 1)
                                fold(BANKS4[2 * j], swi_g[:, j, :])
                                V.tensor_tensor(swi_g[:, j, :], swi_g[:, j, :], rinvh[:], ALU.mult).then_inc(bank_free, 1)
                            if q in (3, 7):
                                dve.wait_ge(tanh_done, f + j + 1)
                                own.mark(V.scalar_tensor_tensor(out=swi_g[:, j, :], in0=swi_t[:, j, :], scalar=1.0,
                                                                in1=swi_g[:, j, :], op0=ALU.add, op1=ALU.mult))
                            if q in (3, 7):
                                dve.wait_ge(w_used, p + 1)
                                if not (first and ph["layer"] == 0 and ph["half"] == 0):
                                    dve.wait_ge(mid_ready, f + j - 1)
                                fold(BANKS4[2 * j + 1], swi_u[:, j, :])
                                V.tensor_tensor(swi_u[:, j, :], swi_u[:, j, :], rinv[:], ALU.mult).then_inc(bank_free, 1)
                                dve.wait_ge(bank_free, g0 + 2 * j + 2)
                                own.need(own.latest())
                                V.tensor_tensor(swi_u[:, j, :], swi_g[:, j, :], swi_u[:, j, :], ALU.mult
                                                ).then_inc(mid_done, 1)
                        if name == "PL":
                            if q in (3, 7):
                                j = q // 4
                                dve.wait_ge(w_used, p + 1)
                                V.tensor_tensor(swi_g[:, j, :], bank[BANKS4[2 * j]][:, 0:SEQ], rinvh[:], ALU.mult
                                                ).then_inc(bank_free, 1)
                            if q in (4, 7):
                                j = 0 if q == 4 else 1
                                m = it * 2 + j
                                done = m + ph["layer"] * KT + 1
                                dve.wait_ge(ple_t, done)
                                V.scalar_tensor_tensor(out=swi_g[:, j, :], in0=swi_t[:, j, :], scalar=1.0,
                                                       in1=bank[BANKS4[2 * j + 1]][:, 0:SEQ], op0=ALU.add, op1=ALU.mult
                                                       ).then_inc(bank_free, 1)
                                dve.wait_ge(bank_free, g0 + 2 * j + 2)
                                V.scalar_tensor_tensor(out=flat(h[:, at(m), :]), in0=swi_g[:, j, :], scalar=0.5,
                                                       in1=flat(h[:, at(m), :]), op0=ALU.mult, op1=ALU.add
                                                       ).then_inc(h_done, 1)
                                if ph["layer"] == 0:
                                    dve.wait_ge(h_done, done)
                                    u_split(3, m, m + 2 * KT + 1, next_u(3))
                        if name == "B1":
                            group = it + ph["half"] * 4
                            very_first = first and ph["half"] == 0
                            if very_first:
                                decay_steps(q)
                            if q == 0 and not first:
                                z_silu(group - 1, 3)
                                group_y(group - 1)
                            if q == 5 and not first:
                                group_var(group - 1)
                            if q == 7 and not first:
                                group_norm(group - 1)
                            if q % 2 == 0 and 2 <= q <= 12:
                                nt = q // 2 - 1
                                dve.wait_ge(conv_t, group * 6 + nt + 1)
                                V.scalar_tensor_tensor(out=ca[:, nt, :], in0=cth[:, nt % 2, :], scalar=1.0,
                                                       in1=ca[:, nt, :], op0=ALU.add, op1=ALU.mult).then_inc(silu_done, 1)
                            if q % 2 == 1:
                                dve.wait_ge(w_used, p + 1)
                                src = bank[BANKS2[q // 2 % 2]][:, 0:SEQ]
                            if q % 2 == 1 and q < 12:
                                nt = q // 2
                                par = lambda k, nt=nt, group=group: flat(bpar[:, at(group), nt * 5 + k:nt * 5 + k + 1])
                                V.tensor_tensor(cpad[:, nt % 2, 3:3 + SEQ], src, rinv[:], ALU.mult).then_inc(bank_free, 1)
                                dve.wait_ge(bank_free, g0 + nt + 1)
                                conv(cpad[:, nt % 2], ca[:, nt, :], par, par(4), None, conv_done)
                            if q % 2 == 1 and q > 12:
                                j = q // 2 - 6
                                if j == 0 and not very_first:
                                    dve.wait_ge(yn_lo, group * 4)
                                V.tensor_tensor(zt[:, j, :], src, rinvh[:], ALU.mult).then_inc(bank_free, 1)
                            if q in (14, 16, 18):
                                z_silu(group, q // 2 - 7)
                            if q == 14:
                                dve.wait_ge(turned, group + 1)
                                own.mark(V.tensor_tensor(cbm, bank[4][:, 0:256].rearrange("p (c l) -> p c l", c=2),
                                                         causal[:].rearrange("p (c l) -> p c l", c=1)
                                                         .broadcast_to([P, 2, CHUNK]), ALU.mult))
                                own.link(V.tensor_copy(btok, bank[4][:, 256:384]))
                                dve.wait_ge(xtok_done, group * 2 + 1)
                                V.tensor_tensor(xdec.rearrange("p (e c) -> p e c", e=GROUP_HEADS),
                                                xtok[:, 0, :].rearrange("p (e c) -> p e c", e=GROUP_HEADS),
                                                wdt[:, at(group * GROUP_HEADS, GROUP_HEADS)]
                                                .rearrange("p (e c) -> p e c", c=1).broadcast_to([P, GROUP_HEADS, 64]),
                                                ALU.mult).then_inc(xdec_done, 1)
                            if q in (15, 17):
                                h0 = 0 if q == 15 else 4
                                dve.wait_ge(exp_done, group * 4 + h0 // 2 + 2)
                                if q == 15:
                                    own.need(own.latest())
                                for e in range(h0, h0 + 4):
                                    for c in range(2):
                                        s = V.scalar_tensor_tensor(
                                            out=csb[:, e, c * CHUNK:(c + 1) * CHUNK], in0=csb[:, e, c * CHUNK:(c + 1) * CHUNK],
                                            scalar=dtt[:, c, at(group * GROUP_HEADS + e)], in1=cbm[:, c, :],
                                            op0=ALU.mult, op1=ALU.mult)
                                s.then_inc(sc_done, 1)

                def z_silu(group, j):
                    dve.wait_ge(z_t, group * 4 + j + 1)
                    own.mark(V.scalar_tensor_tensor(out=zt[:, j, :], in0=cth[:, j % 2, :], scalar=1.0,
                                                    in1=zt[:, j, :], op0=ALU.add, op1=ALU.mult))

                def group_y(group):
                    dsk = lambda j: flat(bpar[:, at(group), 30 + j:31 + j])
                    dve.wait_ge(y_mm, group * 2 + 2)
                    own.need(own.latest())
                    for j in range(4):
                        src = bank[6 if j < 2 else 4][:, (j % 2) * SEQ:(j % 2 + 1) * SEQ]
                        V.scalar_tensor_tensor(out=ca[:, 2 + j, :], in0=ca[:, 2 + j, :], scalar=dsk(j), in1=src,
                                               op0=ALU.mult, op1=ALU.add).then_inc(y_read, 1)
                    for j in range(4):
                        dve.wait_ge(y_read, group * 4 + j + 1)
                        V.tensor_tensor(zt[:, j, :], ca[:, 2 + j, :], zt[:, j, :], ALU.mult).then_inc(yz_done, 1)

                def group_var(group):
                    dve.wait_ge(gstat_mm, group + 1)
                    own.link(V.tensor_scalar(grms[:], bank[7][:, 0:SEQ], 1.0 / 512, EPS, ALU.mult, ALU.add))
                    V.reciprocal(grms[:], grms[:]).then_inc(gvar_done, 1)

                def group_norm(group):
                    dve.wait_ge(grinv_done, group + 1)
                    for j in range(4):
                        V.scalar_tensor_tensor(out=zt[:, j, :], in0=zt[:, j, :], scalar=flat(bpar[:, at(group), 34 + j:35 + j]),
                                               in1=grms[:], op0=ALU.mult, op1=ALU.mult).then_inc(yn_done, 1)

                steps(dve, ph, body, own, {"A1": 26, "B1": 25, "F1": 6, "PL": 0}.get(name, 4))
                own.close()
            dve.wait_ge(h_done, 2 * KT)
            V.tensor_tensor(swi_u[:, 0, :], h[:, KT - 1, :], h[:, KT - 1, :], ALU.mult).then_inc(last_square, 1)
            norm(6)
            for m in range(KT):
                V.scalar_tensor_tensor(out=h[:, m, :], in0=h[:, m, :], scalar=gains[:, 6 * KT + m:6 * KT + m + 1],
                                       in1=rinv[:], op0=ALU.mult, op1=ALU.mult).then_inc(out_ready, 1)

        @block.gpsimd
        def _(pool):
            G = nc.gpsimd
            own = Chain(pool, pool_own)
            G.memset(ones[:], 1.0).then_inc(const_done, 1)
            own.link(G.memset(ident[:], 0.0))
            own.link(G.memset(causal[:], 1.0))
            G.affine_select(out=ident[:], in_=ident[:], compare_op=ALU.not_equal, fill=1.0, base=0,
                            pattern=[[-1, P]], channel_multiplier=1).then_inc(const_done, 1)
            G.affine_select(out=causal[:], in_=causal[:], compare_op=ALU.is_ge, fill=0.0, base=0,
                            pattern=[[1, CHUNK]], channel_multiplier=-1).then_inc(const_done, 1)
            own.close(1)

            def flat(x):
                return x.rearrange("p a t -> p (a t)")

            def clear(norm):
                if norm:
                    pool.wait_ge(stats_done, norm)
                G.memset(sumsq[:], 0.0).then_inc(sumsq_done, 1)

            def add_square(norm, m):
                pool.wait_ge(sumsq_done, m + sumsq_base(norm) + 1)
                own.link(G.tensor_tensor(square[:], flat(h[:, at(m), :]), flat(h[:, at(m), :]), ALU.mult))
                G.tensor_tensor(sumsq[:], sumsq[:], square[:], ALU.add).then_inc(sumsq_done, 1)

            clear(0)
            for m in range(KT // 2):
                if m % 4 == 0:
                    pool.wait_ge(x_in[m // 4], 16)
                add_square(0, m)
            pool.wait_ge(square4_done, 1)
            for m in range(4):
                pool.wait_ge(sumsq_done, KT // 2 + 1 + m)
                G.tensor_tensor(sumsq[:], sumsq[:], square4[:, m, :], ALU.add).then_inc(sumsq_done, 1)
            own.close(1)
            for index, ph in enumerate(phases):
                name = ph["name"]
                norm = next_norm(ph)
                if norm is not None:
                    clear(norm)
                if name == "A1":
                    def lru_split(head, hh):
                        for j in range(2):
                            if j == 1:
                                pool.wait_ge(g_hi, head + 1)
                                G.tensor_tensor(R[1][:, 1, 16:20, :], graw[:, 0:1024].rearrange("p (k t) -> p k t", k=4),
                                                R[1][:, 0, 16:20, :].bitcast(F32), ALU.subtract).then_inc(g_lo, 1)
                            pool.wait_ge(xc_hi, head * 2 + j + 1)
                            G.tensor_tensor(R[1][:, 1, 20 + j, :], xc[:, hh, j, :], R[1][:, 0, 20 + j, :].bitcast(F32),
                                            ALU.subtract).then_inc(xc_lo, 1)

                    def lru_early(head, hh):
                        pool.wait_ge(bank_free, head * 4 + 8)
                        own.link(G.tensor_tensor(ge, yv[:, hh], yv[:, hh], ALU.mult))
                        G.tensor_tensor(ge, ge, yv[:, hh], ALU.mult).then_inc(cube_done, 1)
                        pool.wait_ge(a_done, head * 2 + 2)
                        G.tensor_tensor(sq, av, av, ALU.mult).then_inc(asq_done, 1)

                    def lru_input(head):
                        pool.wait_ge(gated_done, head + 1)
                        pool.wait_ge(mult_done, head + 1)
                        G.tensor_tensor(ti, ti, sq, ALU.mult).then_inc(input_done, 1)

                    def lru_late(head, hh):
                        pool.wait_ge(y_hi, head + 1)
                        for j in range(2):
                            G.tensor_tensor(flat(R[1][:, 1, at(head * 2 + j), :]), yv[:, hh, j, :],
                                            flat(R[1][:, 0, at(head * 2 + j), :]).bitcast(F32), ALU.subtract
                                            ).then_inc(y_lo, 1)

                    def slot(head, hh, first=False):
                        if not first:
                            lru_early(head - 1, 1 - hh)
                        lru_split(head, hh)
                        if not first:
                            lru_input(head - 1)
                            lru_late(head - 1, 1 - hh)

                    slot(0, 0, True)
                    slot(1, 1)
                    own.close()
                    with pool.Fori(1, LRU_HEADS // 2) as it:
                        own.begin(it - 1, 2)
                        slot(it * 2, 0)
                        slot(it * 2 + 1, 1)
                    own.close(LRU_HEADS // 2 - 1)
                    lru_early(LRU_HEADS - 1, 1)
                    lru_input(LRU_HEADS - 1)
                    lru_late(LRU_HEADS - 1, 1)
                    own.close()
                elif name == "F1":
                    f0 = ph["layer"] * FF_TILES + ph["half"] * HALF
                    dst = R[1 - source(ph)]
                    with pool.Fori(0, ph["iters"]) as it:
                        for j in range(2):
                            pool.wait_ge(mid_hi, it * 2 + f0 + j + 1)
                            G.tensor_tensor(flat(dst[:, 1, at(it * 2 + j), :]), swi_u[:, j, :],
                                            flat(dst[:, 0, at(it * 2 + j), :]).bitcast(F32), ALU.subtract
                                            ).then_inc(mid_ready, 1)
                elif name == "B1":
                    g0 = ph["half"] * 4

                    def ce(group):
                        pool.wait_ge(ebc_done, group + 1)
                        pool.wait_ge(silu_done, group * 6 + 2)
                        G.tensor_tensor(ebc, ebc, ca[:, 1:2, CHUNK:SEQ].broadcast_to([P, GROUP_HEADS, CHUNK]), ALU.mult
                                        ).then_inc(ce_done, 1)

                    def y_square(group):
                        for j in range(4):
                            pool.wait_ge(yz_done, group * 4 + j + 1)
                            G.tensor_tensor(ysq[:, j, :], zt[:, j, :], zt[:, j, :], ALU.mult).then_inc(ysq_done, 1)
                        pool.wait_ge(ysq_done, group * 4 + 4)
                        own.link(G.tensor_tensor(ysq[:, 0:2, :], ysq[:, 0:2, :], ysq[:, 2:4, :], ALU.add))
                        G.tensor_tensor(ysq[:, 0, :], ysq[:, 0, :], ysq[:, 1, :], ALU.add).then_inc(ysum_done, 1)

                    def y_split(group, local):
                        for j in range(4):
                            pool.wait_ge(yn_hi, group * 4 + j + 1)
                            G.tensor_tensor(flat(R[0][:, 1, at(local * 4 + j), :]), zt[:, j, :],
                                            flat(R[0][:, 0, at(local * 4 + j), :]).bitcast(F32), ALU.subtract
                                            ).then_inc(yn_lo, 1)
                    ce(g0)
                    own.close()
                    with pool.Fori(1, 4) as it:
                        own.begin(it - 1, 1)
                        y_square(it + (g0 - 1))
                        y_split(it + (g0 - 1), it - 1)
                        ce(it + g0)
                    own.close(3)
                    y_square(g0 + 3)
                    y_split(g0 + 3, 3)
                    own.close()
                if norm is not None:
                    if name == "PL":
                        base = ph["layer"] * KT
                        done = h_done
                    else:
                        base, done = ph["group0"] + 4, bank_free
                    tiles = KT if norm < 6 else KT - 1
                    with pool.Fori(0, tiles) as m:
                        own.begin(m, 1)
                        pool.wait_ge(done, m + base + 1)
                        add_square(norm, m)
                    own.close(tiles)



def blocks_of(w):
    k, m = w.shape
    return w.reshape(k // P, P, m // P, P).transpose(2, 0, 1, 3)


def pieces_of(blocks, widths):
    import numpy as np
    out, b = [], 0
    for w in widths:
        out.append(blocks[:, b:b + w].transpose(0, 2, 1, 3).reshape(blocks.shape[0], -1))
        b += w
    assert b == blocks.shape[1]
    return np.concatenate(out, axis=1)


def halves_first(b):
    it, groups, k = b.shape[:3]
    return b.reshape(it, groups, 2, k // 2, P, P).transpose(0, 2, 1, 3, 4, 5).reshape(it, -1, P, P)


def columns(v):
    return v.reshape(-1, P).T


def lay_out(a):
    import numpy as np
    w = {ph["name"]: ph["widths"] for ph in phase_table()}
    t = {}
    t["xT"] = a["x"][0].T.reshape(KT, P, SEQ).transpose(1, 0, 2)
    t["pT"] = a["p"][:, 0].transpose(0, 2, 1).reshape(2, 2, P, SEQ).transpose(0, 2, 1, 3).reshape(2, P, 2 * SEQ)
    t["gains"] = np.concatenate([columns(a[n][l]) for l in range(2) for n in ("norm_mix_g", "norm_ffn_g", "norm_ple_g")]
                                + [columns(a["final_norm_g"])], axis=1)
    taps = a["a_conv_w"][0].reshape(4, KT, P).transpose(2, 1, 0)
    t["apar"] = np.concatenate([taps] + [columns(v.reshape(-1))[:, :, None] for v in
                                         (a["a_conv_b"], a["a_b_gate_r"], a["a_b_gate_i"], a["a_lambda"])], axis=2)
    order = [[32 + g, 40 + g] + [4 * g + j for j in range(4)] for g in range(GROUPS)]
    conv = np.concatenate([a["b_conv_w"][0], a["b_conv_b"]], axis=0).reshape(5, 48, P).transpose(2, 1, 0)
    conv = conv[:, order].reshape(P, GROUPS, 30)
    dskip = columns(np.repeat(a["b_d_skip"][0], 64)).reshape(P, GROUPS, 4)
    t["bpar"] = np.concatenate([conv, dskip, columns(a["b_norm_g"][0]).reshape(P, GROUPS, 4)], axis=2)
    t["hpar"] = np.stack([a["b_dt_bias"][0], a["b_a_log"][0]], axis=1)
    win = blocks_of(a["a_w_in"][0])
    t["A10"] = pieces_of(np.stack([win[[4 * i, 4 * i + 1, 16 + 4 * i, 17 + 4 * i, 4 * i + 2, 4 * i + 3, 18 + 4 * i,
                                        19 + 4 * i]].reshape(-1, P, P) for i in range(4)]), w["A1"])
    gates = []
    for head in range(LRU_HEADS):
        bs = [blocks_of(a[n][0, head])[m, k] for n in ("a_w_gate_r", "a_w_gate_i") for m in range(2) for k in range(2)]
        gates.append(np.stack(bs, axis=1).reshape(P, 1024))
    t["gates"] = np.stack(gates)
    t["A20"] = pieces_of(halves_first(blocks_of(a["a_w_out"][0]).reshape(4, 4, KT, P, P)), w["A2"])
    bw = a["b_w_in"][0]
    zt, xt = blocks_of(bw[:, :4096]), blocks_of(bw[:, 4096:10240])
    t["B11"] = pieces_of(np.stack([np.concatenate([xt[order[g]], zt[4 * g:4 * g + 4]]).reshape(-1, P, P)
                                   for g in range(GROUPS)]), w["B1"])
    dt = np.concatenate([bw[:, 10240:], bw[:, 10240:]], axis=1)
    t["dtw"] = dt.reshape(KT, P, P).transpose(1, 0, 2).reshape(P, KT * P)
    bo = blocks_of(a["b_w_out"][0])
    t["B21"] = pieces_of(halves_first(bo.reshape(4, 4, 2, 16, P, P).transpose(2, 0, 1, 3, 4, 5).reshape(8, 4, KT, P, P)), w["B2"])
    for l in range(2):
        g, u = blocks_of(a["ffn_w_gate"][l]), blocks_of(a["ffn_w_up"][l])
        t[f"F1{l}"] = pieces_of(np.stack([g, u], axis=1).reshape(FF_TILES // 2, -1, P, P), w["F1"])
        d = blocks_of(a["ffn_w_down"][l])
        t[f"F2{l}"] = pieces_of(d.reshape(4, 4, 2, HALF, P, P).transpose(2, 0, 1, 3, 4, 5).reshape(8, -1, P, P), w["F2"])
        e = np.concatenate([blocks_of(a["ple_w_gate"][l]), blocks_of(a["ple_w_proj"][l])], axis=1)
        t[f"PL{l}"] = pieces_of(e.reshape(8, -1, P, P), w["PL"])
    return {k: np.ascontiguousarray(v) for k, v in t.items()}


def kernel(**inputs):
    import numpy as _np
    import concourse.bacc as _bacc
    from concourse.bass_utils import run_bass_kernel_spmd as _run

    laid = lay_out({k: _np.asarray(v) for k, v in inputs.items()})
    nc = _bacc.Bacc("TRN2", target_bir_lowering=False, num_devices=1)
    arrays = {f"in_{k}": v for k, v in laid.items()}
    t = {k: nc.dram_tensor(f"in_{k}", v.shape, F32, kind="ExternalInput").ap() for k, v in laid.items()}
    out = nc.dram_tensor("out_hT", (P, KT, SEQ), F32, kind="ExternalOutput").ap()
    trunk(nc, t, out)
    got = _run(nc, [arrays], core_ids=[0]).results[0]["out_hT"]
    return _np.ascontiguousarray(got.transpose(1, 0, 2).reshape(D, SEQ).T)[None]
```
